# Optimizing a Trainium2 kernel written in Bass

```python
import math
import jax, jax.numpy as jnp
from jax import lax
import numpy as np

D_MODEL = 1024
BATCH = 1
SEQ = 128
DEPTH = 2
DEC_BATCH = 1
DEC_SEQ = 512
PAST_LEN = 256

GRID_W = 64
N_MIXERS = 2
N_GLA_LAYERS = (DEPTH + 1) // 2
N_DIFF_LAYERS = DEPTH // 2
GLA_HEADS = 4
GLA_DK = D_MODEL // 2 // GLA_HEADS
GLA_DV = D_MODEL // GLA_HEADS
GLA_HK = GLA_HEADS * GLA_DK
GLA_HV = GLA_HEADS * GLA_DV
GLA_RANK = 16
GLA_TAU = 16.0
GLA_CHUNK = 64
DIFF_HEADS = 8
DIFF_DH = D_MODEL // DIFF_HEADS // 2
DIFF_DV = 2 * DIFF_DH
ROPE_THETA = 10000.0
Q_BLOCK = 128
D_FF = (((8 * D_MODEL + 2) // 3 + 255) // 256) * 256
EPS = 1e-6

kernel_name = 'hybrid_gla_diffattn_diffusion_step'

def rmsnorm(x, g):
    x32 = x.astype(jnp.float32)
    y = x32 * lax.rsqrt(jnp.mean(x32 * x32, axis=-1, keepdims=True) + EPS)
    return (y * g.astype(jnp.float32)).astype(x.dtype)

def adaln(cond, w, b):
    m = jax.nn.silu(cond) @ w + b
    return [t[..., None, :] for t in jnp.split(m, 6, axis=-1)]

def axial_rope(n_tokens, dim, dtype):
    rows = n_tokens // GRID_W
    r, col = jnp.meshgrid(jnp.arange(rows), jnp.arange(GRID_W), indexing='ij')
    r = r.reshape(-1).astype(jnp.float32)
    col = col.reshape(-1).astype(jnp.float32)
    n_freq = dim // 4
    inv = ROPE_THETA ** (-jnp.arange(n_freq, dtype=jnp.float32) / n_freq)
    ang = jnp.concatenate([r[:, None] * inv, col[:, None] * inv], axis=-1)
    return jnp.cos(ang).astype(dtype), jnp.sin(ang).astype(dtype)

def apply_rope(x, cos, sin):
    half = x.shape[-1] // 2
    x1, x2 = x[..., :half], x[..., half:]
    cs = cos[None, :, None, None, :]
    sn = sin[None, :, None, None, :]
    return jnp.concatenate([x1 * cs - x2 * sn, x2 * cs + x1 * sn], axis=-1)

def gla_scan(q, k, v, log_a, s0):
    B, T, H, DK = q.shape
    DV = v.shape[-1]
    C = min(GLA_CHUNK, T)
    N = T // C
    f32 = jnp.float32
    q = q.astype(f32).reshape(B, N, C, H, DK) * (DK ** -0.5)
    k = k.astype(f32).reshape(B, N, C, H, DK)
    v = v.astype(f32).reshape(B, N, C, H, DV)
    b = jnp.cumsum(log_a.reshape(B, N, C, H, DK), axis=2)
    b_last = b[:, :, -1]
    q_d = q * jnp.exp(b)
    k_d = k * jnp.exp(-b)
    k_end = k * jnp.exp(b_last[:, :, None] - b)
    mask = jnp.tril(jnp.ones((C, C), dtype=bool))
    A = jnp.where(mask, jnp.einsum('bnthd,bnshd->bnhts', q_d, k_d), 0.0)
    o_intra = jnp.einsum('bnhts,bnshv->bnthv', A, v)
    dS = jnp.einsum('bnshd,bnshv->bnhdv', k_end, v)
    decay = jnp.exp(b_last)

    def step(S, inp):
        dec, ds = inp
        return dec[..., None] * S + ds, S

    s_final, s_in = lax.scan(step, s0.astype(f32), (jnp.moveaxis(decay, 1, 0), jnp.moveaxis(dS, 1, 0)))
    s_in = jnp.moveaxis(s_in, 0, 1)
    o_inter = jnp.einsum('bnthd,bnhdv->bnthv', q_d, s_in)
    return (o_intra + o_inter).reshape(B, T, H, DV), s_final

def gla_mixer(h, s0f, s0b, w_in, w_g1, w_g2, b_g, g_head, w_out):
    B, T, _ = h.shape
    z = h @ w_in
    q = z[..., :GLA_HK].reshape(B, T, GLA_HEADS, GLA_DK)
    k = z[..., GLA_HK:2 * GLA_HK].reshape(B, T, GLA_HEADS, GLA_DK)
    v = z[..., 2 * GLA_HK:2 * GLA_HK + GLA_HV].reshape(B, T, GLA_HEADS, GLA_DV)
    r = z[..., 2 * GLA_HK + GLA_HV:]
    la_f = (jax.nn.log_sigmoid(((h @ w_g1[0]) @ w_g2[0] + b_g[0]).astype(jnp.float32)) / GLA_TAU).reshape(B, T, GLA_HEADS, GLA_DK)
    la_b = (jax.nn.log_sigmoid(((h @ w_g1[1]) @ w_g2[1] + b_g[1]).astype(jnp.float32)) / GLA_TAU).reshape(B, T, GLA_HEADS, GLA_DK)
    o_f, s_f = gla_scan(q, k, v, la_f, s0f)
    o_b, s_b = gla_scan(q[:, ::-1], k[:, ::-1], v[:, ::-1], la_b[:, ::-1], s0b)
    o = rmsnorm(o_f + o_b[:, ::-1], g_head).astype(h.dtype).reshape(B, T, GLA_HV)
    return (o * jax.nn.silu(r)) @ w_out, s_f, s_b

def diff_qkv(h, w_qkv):
    B, T, _ = h.shape
    z = h @ w_qkv
    q = z[..., :D_MODEL].reshape(B, T, DIFF_HEADS, 2, DIFF_DH)
    k = z[..., D_MODEL:2 * D_MODEL].reshape(B, T, DIFF_HEADS, 2, DIFF_DH)
    v = z[..., 2 * D_MODEL:].reshape(B, T, DIFF_HEADS, DIFF_DV)
    return q, k, v

def diff_lambda(lq, lk, lam_init):
    lq = lq.astype(jnp.float32)
    lk = lk.astype(jnp.float32)
    return jnp.exp(jnp.sum(lq[0] * lk[0])) - jnp.exp(jnp.sum(lq[1] * lk[1])) + lam_init

def diff_attend(q, k, v, lam):
    B, Tq = q.shape[:2]
    blk = min(Q_BLOCK, Tq)
    nb = Tq // blk
    qb = jnp.swapaxes(q.reshape(B, nb, blk, DIFF_HEADS, 2, DIFF_DH), 0, 1)

    def one(qi):
        s = jnp.einsum('bqhcd,bkhcd->bhcqk', qi, k).astype(jnp.float32) * (DIFF_DH ** -0.5)
        p = jax.nn.softmax(s, axis=-1)
        w = p[:, :, 0] - lam * p[:, :, 1]
        return jnp.einsum('bhqk,bkhv->bqhv', w.astype(v.dtype), v)

    o = lax.map(one, qb)
    return jnp.swapaxes(o, 0, 1).reshape(B, Tq, DIFF_HEADS, DIFF_DV)

def diff_out(o, g_head, w_out, lam_init):
    B, T = o.shape[:2]
    o = rmsnorm(o, g_head) * (1.0 - lam_init)
    return o.reshape(B, T, DIFF_HEADS * DIFF_DV) @ w_out

def swiglu(h, wg, wu, wd):
    return (jax.nn.silu(h @ wg) * (h @ wu)) @ wd

def setup_inputs(seed: int = 0) -> dict:
    key = jax.random.key(seed)
    ks = iter(jax.random.split(key, 40))
    f32 = jnp.float32

    def nrm(shape, scale):
        return jax.random.normal(next(ks), shape, f32) * scale

    D = D_MODEL
    NG, ND = N_GLA_LAYERS, N_DIFF_LAYERS
    return {
        'x_prompt': nrm((BATCH, SEQ, D), 1.0),
        'x_sample': nrm((DEC_BATCH, DEC_SEQ, D), 1.0),
        'state_gla_fwd': nrm((DEC_BATCH, NG, GLA_HEADS, GLA_DK, GLA_DV), 1.0),
        'state_gla_bwd': nrm((DEC_BATCH, NG, GLA_HEADS, GLA_DK, GLA_DV), 1.0),
        'cache_diff_k': nrm((DEC_BATCH, ND, PAST_LEN, DIFF_HEADS, 2, DIFF_DH), 1.0),
        'cache_diff_v': nrm((DEC_BATCH, ND, PAST_LEN, DIFF_HEADS, DIFF_DV), 1.0),
        'c': nrm((DEC_BATCH, D), 1.0),
        'c_ctx': nrm((D,), 1.0),
        'w_ada': nrm((DEPTH, D, 6 * D), 0.5 * D ** -0.5),
        'b_ada': nrm((DEPTH, 6 * D), 0.01),
        'g_mix_norm': 1.0 + nrm((DEPTH, D), 0.02),
        'g_ffn_norm': 1.0 + nrm((DEPTH, D), 0.02),
        'w_gla_in': nrm((NG, D, 2 * GLA_HK + 2 * GLA_HV), D ** -0.5),
        'w_gla_g1': nrm((NG, 2, D, GLA_RANK), D ** -0.5),
        'w_gla_g2': nrm((NG, 2, GLA_RANK, GLA_HK), GLA_RANK ** -0.5),
        'b_gla_g': nrm((NG, 2, GLA_HK), 0.1),
        'g_gla_head': 1.0 + nrm((NG, GLA_DV), 0.02),
        'w_gla_out': nrm((NG, GLA_HV, D), GLA_HV ** -0.5),
        'w_diff_qkv': nrm((ND, D, 3 * D), D ** -0.5),
        'lam_q': nrm((ND, 2, DIFF_DH), 0.1),
        'lam_k': nrm((ND, 2, DIFF_DH), 0.1),
        'g_diff_head': 1.0 + nrm((ND, DIFF_DV), 0.02),
        'w_diff_out': nrm((ND, DIFF_HEADS * DIFF_DV, D), (DIFF_HEADS * DIFF_DV) ** -0.5),
        'w_ffn_gate': nrm((DEPTH, D, D_FF), D ** -0.5),
        'w_ffn_up': nrm((DEPTH, D, D_FF), D ** -0.5),
        'w_ffn_down': nrm((DEPTH, D_FF, D), D_FF ** -0.5),
        'g_final': 1.0 + nrm((D,), 0.02),
    }

def reference(x_prompt, x_sample, state_gla_fwd, state_gla_bwd, cache_diff_k, cache_diff_v, c, c_ctx,
              w_ada, b_ada, g_mix_norm, g_ffn_norm, w_gla_in, w_gla_g1, w_gla_g2, b_gla_g, g_gla_head,
              w_gla_out, w_diff_qkv, lam_q, lam_k, g_diff_head, w_diff_out, w_ffn_gate, w_ffn_up,
              w_ffn_down, g_final):
    xp, xs = x_prompt, x_sample
    bp = xp.shape[0]
    cos, sin = axial_rope(xs.shape[1], DIFF_DH, xs.dtype)
    new_f, new_b, new_k, new_v = [], [], [], []
    for i in range(DEPTH):
        mp = adaln(c_ctx, w_ada[i], b_ada[i])
        ms = adaln(c, w_ada[i], b_ada[i])
        hp = rmsnorm(xp, g_mix_norm[i]) * (1 + mp[1]) + mp[0]
        hs = rmsnorm(xs, g_mix_norm[i]) * (1 + ms[1]) + ms[0]
        j = i // N_MIXERS
        if i % N_MIXERS == 0:
            gp = (w_gla_in[j], w_gla_g1[j], w_gla_g2[j], b_gla_g[j], g_gla_head[j], w_gla_out[j])
            zero = jnp.zeros((bp, GLA_HEADS, GLA_DK, GLA_DV), jnp.float32)
            op, s_f, s_b = gla_mixer(hp, zero, zero, *gp)
            os_, _, _ = gla_mixer(hs, state_gla_fwd[:, j], state_gla_bwd[:, j], *gp)
            new_f.append(s_f.astype(xp.dtype))
            new_b.append(s_b.astype(xp.dtype))
        else:
            lam_init = 0.8 - 0.6 * math.exp(-0.3 * i)
            lam = diff_lambda(lam_q[j], lam_k[j], lam_init)
            qp, kp, vp = diff_qkv(hp, w_diff_qkv[j])
            qs, ks, vs = diff_qkv(hs, w_diff_qkv[j])
            qs = apply_rope(qs, cos, sin)
            ks = apply_rope(ks, cos, sin)
            op = diff_out(diff_attend(qp, kp, vp, lam), g_diff_head[j], w_diff_out[j], lam_init)
            k_all = jnp.concatenate([cache_diff_k[:, j].astype(ks.dtype), ks], axis=1)
            v_all = jnp.concatenate([cache_diff_v[:, j].astype(vs.dtype), vs], axis=1)
            os_ = diff_out(diff_attend(qs, k_all, v_all, lam), g_diff_head[j], w_diff_out[j], lam_init)
            new_k.append(kp)
            new_v.append(vp)
        xp = xp + mp[2] * op
        xs = xs + ms[2] * os_
        hp = rmsnorm(xp, g_ffn_norm[i]) * (1 + mp[4]) + mp[3]
        hs = rmsnorm(xs, g_ffn_norm[i]) * (1 + ms[4]) + ms[3]
        xp = xp + mp[5] * swiglu(hp, w_ffn_gate[i], w_ffn_up[i], w_ffn_down[i])
        xs = xs + ms[5] * swiglu(hs, w_ffn_gate[i], w_ffn_up[i], w_ffn_down[i])
    y_prompt = rmsnorm(xp, g_final)
    y_sample = rmsnorm(xs, g_final)
    new_state_gla_fwd = jnp.stack(new_f, axis=1)
    new_state_gla_bwd = jnp.stack(new_b, axis=1)
    new_cache_diff_k = jnp.stack(new_k, axis=1)
    new_cache_diff_v = jnp.stack(new_v, axis=1)
    return (y_prompt, y_sample, new_state_gla_fwd, new_state_gla_bwd, new_cache_diff_k, new_cache_diff_v)


_drawn_inputs = setup_inputs


def setup_inputs(seed=0):
    import zlib

    import numpy as np

    out = dict(_drawn_inputs(seed))
    spreads = {}
    factors = {'state_gla_fwd': 8.0,
     'state_gla_bwd': 8.0,
     'g_ffn_norm': 7.358,
     'g_gla_head': 8.0,
     'lam_k': 7.208,
     'g_diff_head': 64.0,
     'g_final': 7.78,
     'cache_diff_k': 3.278}
    for name, (base, spread) in spreads.items():
        noise = np.random.default_rng([zlib.crc32(name.encode()), seed]).standard_normal(out[name].shape)
        drawn = base * np.exp(spread * noise) if base else spread * noise
        out[name] = __import__('jax').numpy.asarray(drawn.astype(out[name].dtype))
    for name, factor in factors.items():
        out[name] = (out[name] * factor).astype(out[name].dtype)
    return out
```

```python
import math
from contextlib import ExitStack

import concourse.bass as bass
from concourse import mybir

F32 = mybir.dt.float32
F32R = mybir.dt.float32r
ALU = mybir.AluOpType
ACT = mybir.ActivationFunctionType
AX_X = mybir.AxisListType.X

P = 128
D = 1024
KD = D // P
NS, NP = 512, 128
T = NS + NP
NT = T // P
HALF = T // 2
EPS = 1e-6
DEPTH = 2

GH, DK, DV = 4, 128, 256
RANK, TAU = 16, 16.0
CH = 64
NCH = T // CH
SCH = NS // CH

AH, DH = 8, 64
PAST = 256
KT = (PAST + T) // P
SK = PAST + NS
LAM_INIT = 0.8 - 0.6 * math.exp(-0.3)

FF = 2816
FT = FF // P
HT = FT // 2
AB = 12

GLA_IN = 0
GLA_OUT = GLA_IN + 3 * GH
FFN = [GLA_OUT + 4, 0]
FHALF = HT + 4
DIF_IN = FFN[0] + 2 * FHALF
DIF_OUT = DIF_IN + 3 * AH // 2
FFN[1] = DIF_OUT + 4
PAIRS = FFN[1] + 2 * FHALF


class Head:

    def __init__(self, i, odd):
        self.i, self.odd, self.n = i, odd, 2 * i + odd
        self.first = isinstance(i, int) and self.n == 0

    def before(self):
        return Head(self.i, 0) if self.odd else Head(self.i - 1, 1)

    def unit(self, j):
        return DIF_IN + 3 * self.i + (3 * self.odd + j) // 2, (3 * self.odd + j) % 2


LAST_HEAD = Head(AH // 2 - 1, 1)


def program(nc, x_prompt, x_sample, state_f, state_b, cache_k, cache_v, c, c_ctx, w_ada, b_ada, g_mix, g_ffn,
            w_in, w_g1, w_g2, b_g, g_head, w_out, w_qkv, lam_q, lam_k, g_dhead, w_dout, w_gate, w_up, w_down,
            g_final, consts, y_prompt, y_sample, new_f, new_b, new_k, new_v):
    ctx = ExitStack()
    with ctx:
        KB = 1024
        base = 4224
        cursor = [base]

        def at(name, shape, dt, offset):
            n = 4
            for s in shape[1:]:
                n *= s
            assert offset + n <= nc.sbuf_usable_end, name
            return nc.alloc_sbuf_tensor_at(name, shape, dt, offset=offset), offset + n

        def keep(name, shape, dt=F32):
            t, cursor[0] = at(name, shape, dt, cursor[0])
            cursor[0] = (cursor[0] + 31) // 32 * 32
            return t

        def psum(name, shape):
            return ctx.enter_context(nc.psum_tensor(name, shape, F32))

        def sem(name):
            return ctx.enter_context(nc.semaphore(name))

        x = keep("x", [P, KD, T])
        h_at = cursor[0]
        h_hi = keep("h_hi", [P, KD, T], F32R)
        h_lo = keep("h_lo", [P, KD, T], F32R)
        raw_at, hi_at, lo_at = ([cursor[0] + (2 * i + s) * 4 * HT * P for s in range(2)] for i in range(3))
        w_raw = [keep(f"w_raw{s}", [P, HT * P]) for s in range(2)]
        w_hi = [keep(f"w_hi{s}", [P, HT * P], F32R) for s in range(2)]
        w_lo = [keep(f"w_lo{s}", [P, HT * P], F32R) for s in range(2)]
        ident = keep("ident", [P, P])
        ones = keep("ones", [P, P])
        mod_bias = keep("mod_bias", [P, 2 * 48])
        vecs = keep("vecs", [P, 67])
        mods = keep("mods", [P, 2 * 48, 2])
        gain = keep("gain", [P, 4, 2, KD])
        cond = keep("cond", [P, KD, 2])
        lam_neg = keep("lam_neg", [P, 1])
        small = keep("small", [P, 64])
        a_raw = [keep(f"a_raw{s}", [P, 2, 512]) for s in range(4)]
        a_row = keep("a_row", [2, 512])
        sq_dump = keep("sq_dump", [P, DV])
        area = cursor[0]

        def carve(start):
            here = [area + start]

            def take(name, shape, dt=F32):
                t, here[0] = at(name, shape, dt, here[0])
                here[0] = (here[0] + 31) // 32 * 32
                return t
            return take

        G_MIX, G_FFN, G_FIN, B_G, G_GH, G_DH, C_S, C_P = 0, 16, 32, 40, 48, 50, 51, 59

        take = carve(0)
        o_buf = take("o_buf", [P, KD, T])
        take = carve(0)
        x_in = take("x_in", [P, NT, D])
        rows_a = take("rows_a", [2 * 48, P])
        rows_b = take("rows_b", [67, P])
        a_first_h, _ = at("a_first_h", [P, 5, 4 * 512], F32, h_at)
        take = carve(53 * KB)
        a_first_x = take("a_first_x", [P, KD - 5, 4 * 512])
        a_first_row = take("a_first_row", [2, 4 * 512])
        take = carve(20 * KB)
        sq_acc = take("sq_acc", [P, T])
        sq = [take(f"sq{s}", [P, T]) for s in range(2)]
        var = take("var", [P, T])
        rstd = take("rstd", [P, T])
        x_n = [take(f"x_n{s}", [P, T]) for s in range(2)]
        h_f = [take(f"h_f{s}", [P, T]) for s in range(2)]
        hid_hi = take("hid_hi", [P, HT, T], F32R)
        hid_lo = take("hid_lo", [P, HT, T], F32R)
        take = carve(0)
        silu_g = take("silu_g", [P, T])
        hid_f = take("hid_f", [P, T])
        take = carve(20 * KB)
        q_t = take("q_t", [P, T])
        k_t = take("k_t", [P, T])
        v_t = take("v_t", [P, T])
        v_tok = take("v_tok", [P, NT, DV])
        r_s = take("r_s", [P, 2, T])
        q_d = [take(f"q_d{d}", [P, T]) for d in range(2)]
        k_d = [take(f"k_d{d}", [P, T]) for d in range(2)]
        k_end = take("k_end", [P, NT, 2, DK])
        attn = take("attn", [P, T])
        state = take("state", [P, 2, 9, DV])
        state0 = take("state0", [P, 2, DV])
        za = [take(f"za{d}", [P, T]) for d in range(2)]
        zb = [take(f"zb{d}", [P, T]) for d in range(2)]
        o_tok = take("o_tok", [P, NT, DV])
        mask = take("mask", [P, 2, P])
        chunk_mask = take("chunk_mask", [P, T])
        z1 = take("z1", [P, T])
        g2 = take("g2", [P, 2, 512])
        g1_raw = take("g1_raw", [P, KD, 2 * RANK])
        g1_hi = take("g1_hi", [P, KD, 2 * RANK], F32R)
        g1_lo = take("g1_lo", [P, KD, 2 * RANK], F32R)
        decay = take("decay", [P, 2, NCH])

        take = carve(20 * KB)
        w_map = [take(f"w_map{s}", [P, SK]) for s in range(2)]
        p1 = [take(f"p1{s}", [P, SK]) for s in range(2)]
        o_f, o_sqr, o_var, o_inv = (take("o_f", [P, T]), take("o_sqr", [P, T]), take("o_var", [P, T]),
                                    take("o_inv", [P, T]))
        take = carve(43 * KB)
        q_hi = take("q_hi", [P, 2, T], F32R)
        q_lo = take("q_lo", [P, 2, T], F32R)
        kk_hi = take("kk_hi", [P, KT * P], F32R)
        kk_lo = take("kk_lo", [P, KT * P], F32R)
        vv_hi = take("vv_hi", [P, KT, P], F32R)
        vv_lo = take("vv_lo", [P, KT, P], F32R)
        q_f, k_f, v_f, roped = (take("q_f", [P, T]), take("k_f", [P, T]), take("v_f", [P, T]), take("roped", [P, NS]))
        wt_hi = [take(f"wt_hi{s}", [P, SK // P, 2 * P], F32R) for s in range(2)]
        wt_lo = [take(f"wt_lo{s}", [P, SK // P, 2 * P], F32R) for s in range(2)]
        stat = take("stat", [P, NT, 10])
        cos_t, sin_t = take("cos_t", [P, NS]), take("sin_t", [P, NS])

        def behind(unit_at, name, shape, dt=F32, skip=0):
            return at(name, shape, dt, unit_at + 4 * (KD + skip) * P)[0]
        k_past, k_new = behind(raw_at[0], "k_past", [P, 2, P]), behind(raw_at[0], "k_new", [P, P], skip=2)
        v_past, v_new = behind(raw_at[1], "v_past", [P, 2, P]), behind(raw_at[1], "v_new", [P, P], skip=2)
        lam_in = behind(hi_at[0], "lam_in", [P, 2, 2 * DH])
        wtp_hi = behind(hi_at[1], "wtp_hi", [P, P], F32R)
        wtp_lo, rot = behind(lo_at[0], "wtp_lo", [P, P], F32R), behind(lo_at[1], "rot", [P, P])
        take = carve(0)
        y_tok = take("y_tok", [P, NT, D])
        take = carve(43 * KB)
        y_t = [take(f"y_t{s}", [P, T]) for s in range(2)]

        acc = [psum(f"acc{s}", [P, 2, 512]) for s in range(2)]
        work = psum("work", [P, 4, 256])
        side = psum("side", [P, 2, 512])
        spare = side[:, 0, :].rearrange("p (r n) -> p r n", r=2)
        misc = side[:, 1, :]
        work2 = work[:, :, :].rearrange("p (b r) n -> p b (r n)", b=2)
        work_t = work[:, :, :].rearrange("p r n -> p (r n)")[:, 0:T]

        raw_in = [sem(f"raw_in{s}") for s in range(2)]
        hi_ready, lo_ready = sem("hi_ready"), sem("lo_ready")
        unit_mm = sem("unit_mm")
        acc_free = [sem(f"acc_free{s}") for s in range(2)]
        a_in = [sem(f"a_in{s}") for s in range(4)]
        a_first_in = [sem(f"a_first_in{k}") for k in range(KD)]
        ada_mm, ada_row, ada_t, ada_mod = sem("ada_mm"), sem("ada_row"), sem("ada_t"), sem("ada_mod")
        gain_ready = sem("gain_ready")
        const_in, row_in, x_land, gla_in_sem = sem("const_in"), sem("row_in"), sem("x_land"), sem("gla_in")
        ones_set, zero_set = sem("ones_set"), sem("zero_set")
        rows_t, vecs_ready, cond_ready = sem("rows_t"), sem("vecs_ready"), sem("cond_ready")
        x_tr, x_ready = sem("x_tr"), sem("x_ready")
        sq_ready, sq_added = sem("sq_ready"), sem("sq_added")
        ss_mm, var_ready, ln_ready, y0_ready, newton = (sem("ss_mm"), sem("var_ready"), sem("ln_ready"),
                                                        sem("y0_ready"), sem("newton"))
        xn_ready, hf_ready, hh_ready, h_ready = sem("xn_ready"), sem("hf_ready"), sem("hh_ready"), sem("h_ready")
        oh_ready, ol_ready = sem("oh_ready"), sem("ol_ready")
        hidh_ready, hidl_ready = sem("hidh_ready"), sem("hidl_ready")
        g1h, g1l, g1_mm, z1_ready = sem("g1h"), sem("g1l"), sem("g1_mm"), sem("z1_ready")
        work_mm, work_free = sem("work_mm"), sem("work_free")
        z_step, log_a, scanned, e_ready = sem("z_step"), sem("log_a"), sem("scanned"), sem("e_ready")
        qd_ready, kd_ready, dec_ready, ke_ready = sem("qd_ready"), sem("kd_ready"), sem("dec_ready"), sem("ke_ready")
        attn_ready = sem("attn_ready")
        ds_mm, st_upd, st_in, st_out = sem("ds_mm"), sem("st_upd"), sem("st_in"), [sem("st_out0"), sem("st_out1")]
        o_sq, on_step, on_act, o_scaled = sem("o_sq"), sem("on_step"), sem("on_act"), sem("o_scaled")
        buf_mm = [sem(f"buf_mm{b}") for b in range(3)]
        buf_free = [sem(f"buf_free{b}") for b in range(3)]
        dif_in, lam_step, lam_ready, q_zero = sem("dif_in"), sem("lam_step"), sem("lam_ready"), sem("q_zero")
        past_in, past_hi, past_lo = sem("past_in"), sem("past_hi"), sem("past_lo")
        rope_step, qs_hi, qs_lo, ks_hi, ks_lo, kc_hi, vt_hi = (sem("rope_step"), sem("qs_hi"), sem("qs_lo"),
                                                               sem("ks_hi"), sem("ks_lo"), sem("kc_hi"), sem("vt_hi"))
        v_out, kv_out, k_out = sem("v_out"), sem("kv_out"), sem("k_out")
        mx_done, nm_ready, ex_ready, rc_step, t_ready, w_ready, wt_up = (
            sem("mx_done"), sem("nm_ready"), sem("ex_ready"), sem("rc_step"), sem("t_ready"), sem("w_ready"),
            sem("wt_up"))
        os_ready, ob_ready = sem("os_ready"), sem("ob_ready")
        y_ready, y_mm, y_copied, y_out = sem("y_ready"), sem("y_mm"), sem("y_copied"), sem("y_out")

        def unit(pair, slot):
            return 2 * pair + slot

        def a_first(k):
            return a_first_h[:, k, :] if k < 5 else a_first_x[:, k - 5, :]

        def cols(w, col, kt=KD):
            return w.rearrange("(k p) n -> p k n", p=P)[:, 0:kt, col]

        w_in0, w_out0, w_qkv0, w_dout0 = w_in[0], w_out[0], w_qkv[0], w_dout[0]

        FIRST_STEPS = ["Zf", "Zb", "Af", "VT0", "Tf", "VT1", "Ab", "Tb"]
        STEPS = ["Zf", "Oa", "Ob", "Zb", "OT0", "Af", "OT1", "VT0", "Tf", "VT1", "Ab", "Tb"]
        LAST_STEPS = ["Oa", "Ob", "OT0", "OT1"]

        def step(h, name):
            if isinstance(h, int) and h == 0:
                return FIRST_STEPS.index(name)
            if isinstance(h, int) and h == GH:
                return len(FIRST_STEPS) + len(STEPS) * (GH - 1) + LAST_STEPS.index(name)
            return len(FIRST_STEPS) - len(STEPS) + len(STEPS) * h + STEPS.index(name)

        DS_F = list(range(SCH - 1)) + [SCH, SCH + 1]
        DS_B = list(range(SCH - 1, 0, -1)) + [SCH + 1, SCH]
        NDS = len(DS_F)

        def state_in(d, n):
            if n >= SCH:
                return None if n == (SCH, SCH + 1)[d] else state[:, d, 7, :]
            if n == (0, SCH - 1)[d]:
                return state0[:, d, :]
            return state[:, d, n - 1 if d == 0 else n, :]

        def state_out(d, n):
            if n >= SCH:
                return state[:, d, 7 if n == (SCH, SCH + 1)[d] else 8, :]
            return state_in(d, n + (1, -1)[d])

        CORE = ["Rq", "Rk", "AD", "VT", "KC", "KT", "AT", "S00",
                "S01", "S10", "S11", "S20", "T0", "S21", "S30", "T1",
                "S31", "O0", "SP", "T2", "T3", "TP", "O1", "SS"]
        buf2 = [work2, side[:, :, :], acc[1][:, :, :]]
        bufs = [b.rearrange("p b n -> p (b n)") for b in buf2]
        NB = len(bufs)

        def buf_of(name):
            return CORE.index(name) % NB

        def count_of(g, name):
            return len(CORE) // NB * g.n + CORE.index(name) // NB

        ADA_TAIL = 10
        ADA_NORM1 = 13
        ADA_NORM2 = 15
        ADA_DIF = 16

        def ada_blocks_of(h):
            return [4 + 2 * h, 5 + 2 * h] if h < 2 else [6 + h]

        block = ctx.enter_context(nc.Block())

        @block.sync
        def _(sp):
            def load(pair, slot, src, kt=KD):
                if not (isinstance(pair, int) and pair == 0):
                    sp.wait_ge(lo_ready, unit(pair, slot) - 1)
                sp.dma_start(w_raw[slot][:, 0:kt * P].rearrange("p (k n) -> p k n", k=kt), src)\
                    .then_inc(raw_in[slot], 16)

            sp.dma_start(x_in[:, 0:NS // P, :], x_sample[0].rearrange("(t p) d -> p t d", p=P)).then_inc(x_land, 16)
            sp.dma_start(x_in[:, NS // P, :], x_prompt[0]).then_inc(x_land, 16)
            sp.dma_start(ident[:, :], consts[:, 0:P]).then_inc(const_in, 16)
            sp.dma_start(rows_b[51:59, :], c.rearrange("b (t p) -> (b t) p", p=P)).then_inc(row_in, 16)
            sp.dma_start(rows_b[59:67, :], c_ctx.rearrange("(t p) -> t p", p=P)).then_inc(row_in, 16)
            sp.dma_start(rows_b[0:16, :], g_mix.rearrange("l (t p) -> (l t) p", p=P)).then_inc(row_in, 16)
            sp.dma_start(rows_b[16:32, :], g_ffn.rearrange("l (t p) -> (l t) p", p=P)).then_inc(row_in, 16)
            sp.dma_start(rows_b[32:40, :], g_final.rearrange("(t p) -> t p", p=P)).then_inc(row_in, 16)
            sp.dma_start(rows_b[40:48, :], b_g[0].rearrange("d (t p) -> (d t) p", p=P)).then_inc(row_in, 16)
            sp.dma_start(rows_b[48:50, :], g_head.rearrange("l (t p) -> (l t) p", p=P)).then_inc(row_in, 16)
            sp.dma_start(rows_b[50:51, :], g_dhead).then_inc(row_in, 16)
            sp.dma_start(rows_a[:, :], b_ada.rearrange("l (t p) -> (l t) p", p=P)).then_inc(row_in, 16)
            for k in range(KD):
                sp.dma_start(a_first(k), w_ada[0, k * P:(k + 1) * P, 0:4 * 512]).then_inc(a_first_in[k], 16)
            load(0, 0, cols(w_in0, slice(0, P)))
            load(0, 1, cols(w_in0, slice(512, 512 + P)))
            for d in range(2):
                sp.dma_start(g1_raw[:, :, d * RANK:(d + 1) * RANK], w_g1[0, d].rearrange("(k p) n -> p k n", p=P))\
                    .then_inc(gla_in_sem, 16)
            sp.wait_ge(zero_set, 1)
            for d in range(2):
                sp.dma_start(g2[d * RANK:(d + 1) * RANK, d, :], w_g2[0, d]).then_inc(gla_in_sem, 16)
            sp.dma_start(mask[:, :, :], consts[:, P:3 * P].rearrange("p (d n) -> p d n", d=2)).then_inc(gla_in_sem, 16)
            sp.dma_start(chunk_mask[:, :], consts[:, 3 * P:3 * P + T]).then_inc(gla_in_sem, 16)

            def gla_head(h, first=False):
                if not first:
                    load(3 * h, 0, cols(w_in0, bass.ds(h * P, P)))
                    load(3 * h, 1, cols(w_in0, bass.ds(512 + h * P, P)))
                load(3 * h + 1, 0, cols(w_in0, bass.ds(1024 + h * DV, P)))
                load(3 * h + 1, 1, cols(w_in0, bass.ds(1024 + P + h * DV, P)))
                load(3 * h + 2, 0, cols(w_in0, bass.ds(2048 + h * DV, P)))
                load(3 * h + 2, 1, cols(w_in0, bass.ds(2048 + P + h * DV, P)))

            gla_head(0, first=True)
            with sp.Fori(1, GH) as h:
                gla_head(h)

            def out_pairs(first, w):
                with sp.Fori(0, KD // 2) as i:
                    for s in range(2):
                        load(first + i, s, cols(w, bass.ds(i * 2 * P + s * P, P)))

            def ffn(layer):
                for half in range(2):
                    first = FFN[layer] + half * FHALF
                    with sp.Fori(0, HT) as i:
                        load(first + i, 0, cols(w_gate[layer], bass.ds(i * P + half * HT * P, P)))
                        load(first + i, 1, cols(w_up[layer], bass.ds(i * P + half * HT * P, P)))
                    down = w_down[layer, half * HT * P:(half + 1) * HT * P, :]
                    with sp.Fori(0, KD // 2) as i:
                        for s in range(2):
                            load(first + HT + i, s, cols(down, bass.ds(i * 2 * P + s * P, P), HT), HT)

            out_pairs(GLA_OUT, w_out0)
            ffn(0)
            with sp.Fori(0, AH // 2) as i:
                for odd in range(2):
                    for j in range(3):
                        load(*Head(i, odd).unit(j), cols(w_qkv0, bass.ds(i * 2 * P + odd * P + j * D, P)))
            out_pairs(DIF_OUT, w_dout0)
            sp.wait_ge(kv_out, 16 * AH)
            sp.wait_ge(k_out, 16 * AH)
            ffn(1)
            for k in range(KD):
                sp.wait_ge(y_copied, 2 * k + 2)
                sp.dma_start(y_sample[0].rearrange("(t p) d -> p t d", p=P)[:, :, k * P:(k + 1) * P],
                             y_tok[:, 0:NS // P, k * P:(k + 1) * P]).then_inc(y_out, 16)
                sp.dma_start(y_prompt[0][:, k * P:(k + 1) * P], y_tok[:, NS // P, k * P:(k + 1) * P])\
                    .then_inc(y_out, 16)
            sp.wait_ge(y_out, 16 * 2 * KD)

        @block.gpsimd
        def _(pool):
            def ada_block(b):
                layer = b // AB
                wl = w_ada[layer].rearrange("(k p) n -> p k n", p=P)
                for q in range(4):
                    if b > 4:
                        pool.wait_ge(ada_mm, 4 * b + q - 3)
                    pool.dma_start(a_raw[q][:, :, :], wl[:, 2 * q:2 * q + 2, bass.ds(b % AB * 512, 512)])\
                        .then_inc(a_in[q], 16)

            pool.memset(g2[:, :, :], 0.0).then_inc(zero_set, 1)
            pool.memset(z1[:, :], 0.0).then_inc(zero_set, 1)
            pool.memset(k_end[:, :, :, :], 0.0).then_inc(zero_set, 1)
            for h in range(GH):
                blocks = ada_blocks_of(h)
                if h == 0:
                    pool.wait_ge(a_first_in[KD - 1], 16)
                ada_block(blocks[0])
                if h >= 1:
                    pool.wait_ge(work_mm, step(h, "Ob") + 1)
                else:
                    pool.wait_ge(ada_mod, 4)
                pool.dma_start(state0[:, 0, :], state_f[0, 0, h]).then_inc(st_in, 16)
                pool.dma_start(state0[:, 1, :], state_b[0, 0, h]).then_inc(st_in, 16)
                if h >= 1:
                    for d, dst in ((0, new_f), (1, new_b)):
                        pool.wait_ge(st_upd, 2 * NDS * (h - 1) + NDS * (d + 1))
                        pool.dma_start(dst[0, 0, h - 1], state[:, d, 8, :]).then_inc(st_out[d], 16)
                for b in blocks[1:]:
                    ada_block(b)
            ada_block(ADA_TAIL)
            for d, dst in ((0, new_f), (1, new_b)):
                pool.wait_ge(st_upd, 2 * NDS * (GH - 1) + NDS * (d + 1))
                pool.dma_start(dst[0, 0, GH - 1], state[:, d, 8, :]).then_inc(st_out[d], 16)
            for b in range(ADA_TAIL + 1, ADA_DIF + 1):
                ada_block(b)
            pool.wait_ge(unit_mm, unit(DIF_IN, 0))
            for dst, a in ((rot, 3 * P + T), (cos_t, 4 * P + T), (sin_t, 4 * P + T + NS)):
                pool.dma_start(dst[:, :], consts[:, a:a + dst.shape[1]]).then_inc(dif_in, 16)
            for i, src in enumerate((lam_q, lam_k)):
                pool.dma_start(lam_in[:, i, :], src.rearrange("a m d -> a (m d)").partition_broadcast(P))\
                    .then_inc(dif_in, 16)
            for t in (q_hi, q_lo):
                pool.memset(t[CH:P, 0, :].bitcast(F32), 0.0).then_inc(q_zero, 1)
                pool.memset(t[0:CH, 1, :].bitcast(F32), 0.0).then_inc(q_zero, 1)

            def cache_tiles(g):
                if not g.first:
                    pool.wait_ge(buf_mm[buf_of("KC")], count_of(g.before(), "KC") + 1)
                    pool.wait_ge(past_lo, g.n)
                h = bass.ds(g.n, 1)
                pool.dma_start(k_past[:, :, :], cache_k[0, 0, :, h].rearrange("(t p) a m d -> p t (a m d)", p=P))\
                    .then_inc(past_in, 16)
                pool.dma_start(v_past[:, :, :], cache_v[0, 0, :, h].rearrange("(t p) a d -> p t (a d)", p=P))\
                    .then_inc(past_in, 16)
                pool.wait_ge(v_out, g.n + 1)
                pool.dma_start(new_v[0, 0, :, h].rearrange("t a d -> t (a d)"), v_new[:, :]).then_inc(kv_out, 16)
                pool.wait_ge(buf_free[buf_of("KT")], count_of(g, "KT") + 1)
                pool.dma_start(new_k[0, 0, :, h].rearrange("t a m d -> t (a m d)"), k_new[:, :]).then_inc(k_out, 16)

            def next_ada(g):
                pool.wait_ge(buf_free[buf_of("AD")], count_of(g, "AD") + 1)
                for q in range(4):
                    pool.dma_start(a_raw[q][:, :, :], w_ada[1].rearrange("(k p) n -> p k n", p=P)
                                   [:, 2 * q:2 * q + 2, bass.ds((g.n + ADA_DIF + 1 - AB) * 512, 512)]).then_inc(a_in[q], 16)
            for n in range(AH):
                g = Head(n // 2, n % 2)
                cache_tiles(g)
                if n < AH - 1:
                    next_ada(g)
            pool.wait_ge(kv_out, 16 * AH)
            pool.wait_ge(k_out, 16 * AH)
            for d in range(2):
                pool.wait_ge(st_out[d], 16 * GH)

        @block.tensor
        def _(pe):
            def tile_products(slot, k, kt, hi, lo, out=None):
                out = acc[slot] if out is None else out
                for n, (w, a) in enumerate(((w_hi, hi), (w_hi, lo), (w_lo, hi))):
                    for s in range(2):
                        mm = pe.matmul(out[:, s, 0:HALF], w[slot][:, k * P:(k + 1) * P],
                                       a(k)[:, s * HALF:(s + 1) * HALF],
                                       start=(k == 0 and n == 0), stop=(k == kt - 1 and n == 2))
                return mm

            def gemm(pair, slot, kt, hi, lo, gaps={}, arrive=None):
                pe.wait_ge(lo_ready, unit(pair, slot) + 1)
                if not (isinstance(pair, int) and pair == 0):
                    pe.wait_ge(acc_free[slot], pair)
                for k in range(kt):
                    if arrive:
                        arrive(k)
                    mm = tile_products(slot, k, kt, hi, lo)
                    if k == kt - 1:
                        mm.then_inc(unit_mm, 1)
                    for f in gaps.get(k, ()):
                        f()

            def gemm_both(pair, arrive, gaps={}):
                pe.wait_ge(lo_ready, unit(pair, 1) + 1)
                for slot in range(2):
                    pe.wait_ge(acc_free[slot], pair)
                for k in range(KD):
                    arrive(k)
                    for slot in range(2):
                        mm = tile_products(slot, k, KD, h_hi_k, h_lo_k)
                        if k == KD - 1:
                            mm.then_inc(unit_mm, 1)
                    for f in gaps.get(k, ()):
                        f()

            def h_hi_k(k):
                return h_hi[:, k, :]

            def h_lo_k(k):
                return h_lo[:, k, :]

            def ada_chunk(b, q, out=misc):
                if q == 0 and out is misc:
                    pe.wait_ge(ada_mod, b)
                pe.wait_ge(a_in[q], 16 * (b - 3))
                for j in range(2):
                    mm = pe.matmul(out[0:2, 0:512], cond[:, 2 * q + j, :], a_raw[q][:, j, :],
                                   start=(q == 0 and j == 0), stop=(q == 3 and j == 1))
                return mm.then_inc(ada_mm, 1) if out is misc else mm

            def ada_turn(b):
                pe.wait_ge(ada_row, b + 1)
                turn_rows(misc, a_row, 4).then_inc(ada_t, 1)

            def turn_rows(out, row, tiles):
                for j in range(tiles):
                    mm = pe.matmul(out[:, 2 * j:2 * j + 2], row[0:2, j * P:(j + 1) * P], ident[0:2, 0:2],
                                   start=True, stop=True)
                return mm

            pe.wait_ge(const_in, 16)
            pe.wait_ge(row_in, 16 * 9)
            pe.transpose(misc[:, 0:96], rows_a[:, :], ident[0:96, 0:96]).then_inc(rows_t, 1)
            pe.transpose(misc[:, 128:128 + 67], rows_b[:, :], ident[0:67, 0:67]).then_inc(rows_t, 1)
            def sum_squares(n, out=work2):
                pe.wait_ge(sq_added, (KD - 2) * (n + 1))
                for part, squares in enumerate((sq_acc, sq[(KD - 1) % 2])):
                    if part:
                        pe.wait_ge(sq_ready, KD * (n + 1))
                    for s in range(2):
                        mm = pe.matmul(out[:, s, 0:HALF], ones[:, :], squares[:, s * HALF:(s + 1) * HALF],
                                       start=(part == 0), stop=(part == 1))
                mm.then_inc(ss_mm, 1)

            def x_turn(k):
                if k >= 2:
                    pe.wait_ge(x_ready, 2 * (k - 1))
                for t in range(NT):
                    mm = pe.transpose(acc[k % 2][:, t // 4, (t % 4) * P:(t % 4 + 1) * P],
                                      x_in[:, t, k * P:(k + 1) * P], ident[:, :])
                mm.then_inc(x_tr, 1)

            first_rows = [work2[0:2, 0, :], work2[0:2, 1, :], side[0:2, 0, :], side[0:2, 1, :]]

            def ada_first(k):
                if k == 0:
                    pe.wait_ge(cond_ready, 1)
                    pe.wait_ge(vecs_ready, 2)
                pe.wait_ge(a_first_in[k], 16)
                for b in range(4):
                    mm = pe.matmul(first_rows[b], cond[:, k, :], a_first(k)[:, b * 512:(b + 1) * 512],
                                   start=(k == 0), stop=(k == KD - 1))
                if k == KD - 1:
                    mm.then_inc(ada_mm, 16)

            pe.wait_ge(x_land, 32)
            for k in range(KD):
                x_turn(k)
                if k >= 2:
                    ada_first(k - 2)
            ada_first(KD - 2)
            ada_first(KD - 1)
            pe.wait_ge(ones_set, 1)
            sum_squares(0, acc[0])
            pe.wait_ge(ada_row, 4)
            turn_rows(acc[1][:, 0, :], a_first_row, 16).then_inc(ada_t, 4)

            def gates(h, d, name):
                if not (isinstance(h, int) and h == 0 and d == 0):
                    pe.wait_ge(work_free, step(h, name))
                for s in range(2):
                    mm = pe.matmul(work2[:, s, 0:HALF], g2_head(h, d), z1[:, s * HALF:(s + 1) * HALF],
                                   start=True, stop=True)
                mm.then_inc(work_mm, 1)

            def g2_head(h, d):
                return g2[:, d, h * DK:(h + 1) * DK]

            def five(h, name, pieces):
                pe.wait_ge(work_free, step(h, name))
                for t in range(NT):
                    mm = pe.transpose(work_t[:, t * P:(t + 1) * P], pieces(t), ident[:, :])
                mm.then_inc(work_mm, 1)

            def scores(h, d, name):
                pe.wait_ge(kd_ready, 2 * h + d + 1)
                pe.wait_ge(qd_ready, 2 * h + d + 1)
                pe.wait_ge(work_free, step(h, name))
                for t in range(NT):
                    mm = pe.matmul(work_t[:, t * P:(t + 1) * P], k_d[d][:, t * P:(t + 1) * P],
                                   q_d[d][:, t * P:(t + 1) * P], start=True, stop=True)
                mm.then_inc(work_mm, 1)

            def k_end_turn(h, d, name):
                pe.wait_ge(ke_ready, 2 * h + d + 1)
                five(h, name, lambda t: za[d][:, t * P:(t + 1) * P])

            def v_turn(h, j, name):
                pe.wait_ge(acc_free[j], 3 * h + 2)
                five(h, name, lambda t: v_t[:, t * P:(t + 1) * P])

            def kv_sums(h, d, batch):
                pe.wait_ge(work_free, step(h, ("Tf", "Tb")[d]) + 1)
                pe.wait_ge(work_free, step(h, "VT1") + 1)
                for i in range(2 * batch, min(2 * batch + 2, NDS)):
                    n = (DS_F, DS_B)[d][i]
                    number = 2 * NDS * h + NDS * d + 2 * batch
                    if number:
                        pe.wait_ge(st_upd, number)
                    mm = pe.matmul(spare[:, i % 2, :], k_end[:, n // 2, n % 2, :], v_tok[:, n // 2, :],
                                   start=True, stop=True)
                mm.then_inc(ds_mm, 1)

            def outputs(h, part):
                pe.wait_ge(attn_ready, h)
                pe.wait_ge(st_upd, 2 * NDS * h)
                pe.wait_ge(st_in, 32 * h)
                pe.wait_ge(work_free, step(h, "Oa" if part == 0 else "Ob"))
                for t in (range(4) if part == 0 else (4,)):
                    r = t % 4
                    inter = [(d, cc) for d in range(2) for cc in range(2) if state_in(d, 2 * t + cc) is not None]
                    pe.matmul(work[:, r, :], attn[:, t * P:(t + 1) * P], v_tok[:, t, :], start=True, stop=False,
                              skip_group_check=True)
                    for i, (d, cc) in enumerate(inter):
                        mm = pe.matmul(work[cc * CH:(cc + 1) * CH, r, :],
                                       q_d[d][:, t * P + cc * CH:t * P + (cc + 1) * CH],
                                       state_in(d, 2 * t + cc), start=False, stop=(i == len(inter) - 1),
                                       skip_group_check=True)
                mm.then_inc(work_mm, 1)

            def o_turn(h, j, name):
                pe.wait_ge(o_scaled, h)
                five(h, name, lambda t: o_tok[:, t, j * P:(j + 1) * P])

            pe.wait_ge(g1l, 1)
            pe.wait_ge(lo_ready, 1)
            for k in range(KD):
                pe.wait_ge(h_ready, k + 1)
                head_q = tile_products(0, k, KD, h_hi_k, h_lo_k)
                for n, (w, a) in enumerate(((g1_hi, h_hi), (g1_hi, h_lo), (g1_lo, h_hi))):
                    for s in range(2):
                        mm = pe.matmul(acc[1][0:2 * RANK, s, 0:HALF], w[:, k, :], a[:, k, s * HALF:(s + 1) * HALF],
                                       start=(k == 0 and n == 0), stop=(k == KD - 1 and n == 2))
            head_q.then_inc(unit_mm, 1)
            mm.then_inc(g1_mm, 1)
            pe.wait_ge(z1_ready, 1)

            def gla_head(h):
                first = isinstance(h, int) and h == 0

                def old(f):
                    return [] if first else [f]
                blocks = ada_blocks_of(h)
                ada = [[lambda q=q, b=b: ada_chunk(b, q) if b else None for q in range(4)] for b in (blocks + [None])[:2]]
                turns = [lambda b=b: ada_turn(b) if b else None for b in (blocks + [None])[:2]]
                gaps = {0: old(lambda: kv_sums(h - 1, 1, 0)), 2: old(lambda: kv_sums(h - 1, 1, 1)),
                        3: [lambda: gates(h, 0, "Zf")], 4: old(lambda: kv_sums(h - 1, 1, 2)),
                        5: [ada[0][0]] + old(lambda: kv_sums(h - 1, 1, 3)),
                        6: [ada[0][1]] + old(lambda: kv_sums(h - 1, 1, 4)), 7: old(lambda: outputs(h, 0))}
                if first:
                    for k in range(KD):
                        for f in gaps.get(k, ()):
                            f()
                else:
                    gemm(3 * h, 0, KD, h_hi_k, h_lo_k, gaps)
                gemm(3 * h, 1, KD, h_hi_k, h_lo_k,
                     {3: old(lambda: outputs(h, 1)) + [ada[0][2]], 5: [ada[0][3]], 7: [lambda: gates(h, 1, "Zb")]})
                gemm(3 * h + 1, 0, KD, h_hi_k, h_lo_k,
                     {3: [turns[0]], 7: old(lambda: o_turn(h, 0, "OT0"))})
                gemm(3 * h + 1, 1, KD, h_hi_k, h_lo_k,
                     {1: [ada[1][0]], 3: [lambda: scores(h, 0, "Af")], 5: [ada[1][1]],
                      7: old(lambda: o_turn(h, 1, "OT1"))})
                gemm(3 * h + 2, 0, KD, h_hi_k, h_lo_k,
                     {1: [lambda: v_turn(h, 0, "VT0")], 3: [ada[1][2]],
                      4: [lambda: k_end_turn(h, 0, "Tf")], 6: [ada[1][3]]})
                gemm(3 * h + 2, 1, KD, h_hi_k, h_lo_k,
                     {0: [lambda: v_turn(h, 1, "VT1")], 2: [lambda: kv_sums(h, 0, 0)], 3: [lambda: kv_sums(h, 0, 1)],
                      4: [lambda: scores(h, 1, "Ab"), lambda: kv_sums(h, 0, 2)],
                      5: [lambda: kv_sums(h, 0, 3)], 6: [turns[1], lambda: kv_sums(h, 0, 4)],
                      7: [lambda: k_end_turn(h, 1, "Tb")]})

            for h in range(GH):
                gla_head(h)
            for batch in range((NDS + 1) // 2):
                kv_sums(GH - 1, 1, batch)
                if batch < 4:
                    ada_chunk(ADA_TAIL, batch)
            outputs(GH, 0)
            ada_turn(ADA_TAIL)
            outputs(GH, 1)
            for q in range(4):
                ada_chunk(ADA_TAIL + 1, q)
            o_turn(GH, 0, "OT0")
            o_turn(GH, 1, "OT1")
            ada_turn(ADA_TAIL + 1)
            for q in range(4):
                ada_chunk(ADA_TAIL + 2, q)

            def projection(first, l, extra=()):
                def one(i, peel):
                    def arrive(k):
                        pe.wait_ge(ol_ready, KD * l + k + 1)
                    gemm(first + i, 0, KD, h_hi_k, h_lo_k, {}, arrive if peel else None)
                    gemm(first + i, 1, KD, h_hi_k, h_lo_k, {0: extra} if peel else {})
                one(0, True)
                with pe.Fori(1, KD // 2) as i:
                    one(i, False)

            def ffn(layer, n, beside=None):
                for half in range(2):
                    first = FFN[layer] + half * FHALF
                    if half == 0:
                        gaps = {k: [lambda q=q: ada_chunk(beside, q)] for q, k in enumerate((0, 2, 4, 6))} if beside else {}
                        gemm_both(first, lambda k: pe.wait_ge(h_ready, KD * n + k + 1), gaps)
                        if beside:
                            ada_turn(beside)
                    with pe.Fori(1 - half, HT) as i:
                        gemm(first + i, 0, KD, h_hi_k, h_lo_k)
                        gemm(first + i, 1, KD, h_hi_k, h_lo_k)

                    def down(i, peel):
                        def arrive(k):
                            pe.wait_ge(hidl_ready, HT * (2 * layer + half) + k + 1)
                        for slot in range(2):
                            gemm(first + HT + i, slot, HT, lambda k: hid_hi[:, k, :], lambda k: hid_lo[:, k, :], {},
                                 arrive if peel and slot == 0 else None)
                    down(0, True)
                    with pe.Fori(1, KD // 2) as i:
                        down(i, False)

            def ada_whole(b):
                for q in range(4):
                    ada_chunk(b, q)
                ada_turn(b)

            projection(GLA_OUT, 0, [lambda: ada_turn(ADA_TAIL + 2)])
            sum_squares(1)
            ada_whole(ADA_NORM1)
            ffn(0, 1, ADA_NORM1 + 1)
            sum_squares(2)
            ada_whole(ADA_NORM2)

            def begin(g, name):
                b = buf_of(name)
                if not (g.first and count_of(g, name) == 0):
                    pe.wait_ge(buf_free[b], count_of(g, name))
                return bufs[b]

            def split_mul(out, whi, wlo, ahi, alo, start=True, stop=True):
                pe.matmul(out, whi, ahi, start=start, stop=False)
                pe.matmul(out, whi, alo, start=False, stop=False)
                return pe.matmul(out, wlo, ahi, start=False, stop=stop)

            def rotate(g, name, src):
                j = 0 if src is q_f else 1
                pair, slot = g.unit(j)
                out = begin(g, name)
                pe.wait_ge(acc_free[slot], pair + 1)
                if g.first:
                    pe.wait_ge(dif_in, 16 * 5)
                pe.matmul(out[:, 0:NS], rot[:, :], src[:, 0:NS], start=True, stop=True).then_inc(buf_mm[buf_of(name)], 1)

            def turn(g, name, tiles):
                out = begin(g, name)
                for t, tile in enumerate(tiles):
                    mm = pe.transpose(out[:, t * P:(t + 1) * P], tile, ident[:, :])
                mm.then_inc(buf_mm[buf_of(name)], 1)

            def prepare(g):
                pair, slot = g.unit(2)

                def v_turn():
                    pe.wait_ge(acc_free[slot], pair + 1)
                    turn(g, "VT", [v_f[:, t * P:(t + 1) * P] for t in range(NT)])

                def k_turn():
                    pe.wait_ge(past_in, 32 * (g.n + 1))
                    turn(g, "KC", [k_past[:, t, :] for t in range(2)])

                def ada_rows():
                    out = begin(g, "AD")
                    for q in range(4):
                        mm = ada_chunk(ADA_DIF + g.n, q, out)
                    mm.then_inc(buf_mm[buf_of("AD")], 1)

                def ada_columns():
                    out = begin(g, "AT")
                    pe.wait_ge(buf_free[buf_of("AD")], count_of(g, "AD") + 1)
                    turn_rows(out, a_row, 4).then_inc(buf_mm[buf_of("AT")], 1)
                return {0: [lambda: rotate(g, "Rq", q_f)], 1: [lambda: rotate(g, "Rk", k_f)], 2: [ada_rows],
                        3: [v_turn], 4: [k_turn], 5: [lambda: turn(g, "KT", [k_f[:, NS:T]])], 6: [ada_columns]}

            def logits(g, q, m):
                name = f"S{q}{m}"
                out = begin(g, name)
                if q == 0 and m == 0:
                    pe.wait_ge(qs_lo, 2 * g.n + 2)
                    pe.wait_ge(ks_lo, g.n + 1)
                    pe.wait_ge(buf_free[buf_of("KC")], count_of(g, "KC") + 1)
                for a, b in ((0, 512), (512, SK)):
                    mm = split_mul(out[:, a:b], q_hi[:, m, q * P:(q + 1) * P], q_lo[:, m, q * P:(q + 1) * P],
                                   kk_hi[:, a:b], kk_lo[:, a:b])
                mm.then_inc(buf_mm[buf_of(name)], 1)

            def prompt_logits(g):
                out = begin(g, "SP")
                for m in range(2):
                    mm = split_mul(out[:, m * P:(m + 1) * P], q_hi[:, m, NS:T], q_lo[:, m, NS:T],
                                   kk_hi[:, SK:SK + P], kk_lo[:, SK:SK + P])
                mm.then_inc(buf_mm[buf_of("SP")], 1)

            def w_turn(g, q):
                pe.wait_ge(w_ready, NT * g.n + q + 1)
                if q < 4:
                    turn(g, f"T{q}", [w_map[q % 2][:, t * P:(t + 1) * P] for t in range(SK // P)])
                else:
                    turn(g, "TP", [w_map[0][:, 0:P]])

            def values(g, pp):
                name = f"O{pp}"
                out = begin(g, name)
                pe.wait_ge(buf_free[buf_of(f"T{2 * pp + 1}")], count_of(g, f"T{2 * pp + 1}") + 1)
                if pp == 0:
                    pe.wait_ge(past_lo, g.n + 1)
                    pe.wait_ge(buf_free[buf_of("VT")], count_of(g, "VT") + 1)
                for t in range(SK // P):
                    mm = split_mul(out[:, 0:2 * P], vv_hi[:, t, :], vv_lo[:, t, :], wt_hi[pp][:, t, :], wt_lo[pp][:, t, :],
                                   start=(t == 0), stop=(t == SK // P - 1))
                if pp:
                    pe.wait_ge(buf_free[buf_of("TP")], count_of(g, "TP") + 1)
                    mm = split_mul(out[:, 512:512 + P], vv_hi[:, KT - 1, :], vv_lo[:, KT - 1, :], wtp_hi[:, :], wtp_lo[:, :])
                mm.then_inc(buf_mm[buf_of(name)], 1)

            def o_squares_sum(g):
                begin(g, "SS")
                pe.wait_ge(os_ready, g.n + 1)
                out = buf2[buf_of("SS")]
                for s in range(2):
                    mm = pe.matmul(out[:, s, 0:HALF], ones[:, :], o_sqr[:, s * HALF:(s + 1) * HALF], start=True, stop=True)
                mm.then_inc(buf_mm[buf_of("SS")], 1)

            def core(g):
                def s(q, m):
                    return [lambda: logits(g, q, m)]

                def t(q):
                    return [lambda: w_turn(g, q)]
                first = prepare(g)
                first[7] = s(0, 0)
                return [first,
                        {0: s(0, 1), 1: s(1, 0), 2: s(1, 1), 3: s(2, 0), 4: t(0), 5: s(2, 1), 6: s(3, 0), 7: t(1)},
                        {0: s(3, 1), 1: [lambda: values(g, 0)], 2: [lambda: prompt_logits(g)], 3: t(2), 4: t(3),
                         5: t(4), 6: [lambda: values(g, 1)], 7: [lambda: o_squares_sum(g)]}]

            gemm_both(DIF_IN, lambda k: pe.wait_ge(h_ready, KD * 2 + k + 1))

            def dif_gemm(h, j, gaps):
                pair, slot = h.unit(j)
                pe.wait_ge(lo_ready, unit(pair, slot) + 1)
                if h.first or slot == 0:
                    pe.wait_ge(acc_free[0 if h.first else 1], pair)
                else:
                    pe.wait_ge(acc_free[0], pair + 1)
                for k in range(KD):
                    mm = tile_products(slot, k, KD, h_hi_k, h_lo_k, acc[0])
                    if k == KD - 1:
                        mm.then_inc(unit_mm, 1)
                    for f in gaps.get(k, ()):
                        f()
            dif_gemm(Head(0, 0), 2, {})
            pe.wait_ge(acc_free[1], DIF_IN + 1)

            def head_products(h):
                for j, gaps in enumerate(core(h.before())):
                    dif_gemm(h, j, gaps)
            head_products(Head(0, 1))
            with pe.Fori(1, AH // 2) as i:
                for odd in range(2):
                    head_products(Head(i, odd))
            for gaps in core(LAST_HEAD):
                for k in range(KD):
                    for f in gaps[k]:
                        f()
            pe.wait_ge(buf_free[buf_of("SS")], count_of(LAST_HEAD, "SS") + 1)
            projection(DIF_OUT, 1)
            sum_squares(3)
            ffn(1, 3)
            sum_squares(4)
            for k in range(KD):
                pe.wait_ge(y_ready, k + 1)
                if k >= 2:
                    pe.wait_ge(y_copied, 2 * k - 2)
                for t in range(NT):
                    mm = pe.transpose(acc[k % 2][:, t // 4, (t % 4) * P:(t % 4 + 1) * P], y_t[k % 2][:, t * P:(t + 1) * P],
                                      ident[:, :])
                mm.then_inc(y_mm, 1)

        @block.scalar
        def _(act):
            def split_hi(pair, slot, kt=KD):
                act.wait_ge(raw_in[slot], 16 * (pair + 1))
                if not (isinstance(pair, int) and pair == 0):
                    act.wait_ge(unit_mm, unit(pair, slot) - 1)
                act.activation(w_hi[slot][:, 0:kt * P], w_raw[slot][:, 0:kt * P], ACT.Copy).then_inc(hi_ready, 1)

            def squares(n, k, avail):
                avail()
                if k == 0:
                    if n:
                        act.wait_ge(ss_mm, n)
                    act.activation(sq_acc[:, :], x[:, k, :], ACT.Square).then_inc(sq_ready, 1)
                else:
                    if k >= 3:
                        act.wait_ge(sq_added, (KD - 2) * n + k - 2)
                    act.activation(sq[k % 2][:, :], x[:, k, :], ACT.Square).then_inc(sq_ready, 1)

            def norm_inv_sqrt(m, n):
                act.wait_ge(var_ready, n + 1)
                inv_sqrt(m, var[:, :], rstd[:, :])

            def inv_sqrt(m, v, y):
                act.activation(y, v, ACT.Ln).then_inc(ln_ready, 1)
                act.wait_ge(ln_ready, m + 1)
                act.activation(y, y, ACT.Exp, scale=-0.5).then_inc(y0_ready, 1)

            def modulate(n):
                l, part = n // 2, n % 2
                act.wait_ge(gain_ready, 2 * (n + 1))
                for k in range(KD):
                    sh = l * 48 + (3 * part) * 8 + k
                    act.wait_ge(xn_ready, KD * n + k + 1)
                    if k >= 2:
                        act.wait_ge(h_ready, KD * n + k - 1)
                    act.activation(h_f[k % 2][:, 0:NS], x_n[k % 2][:, 0:NS], ACT.Identity,
                                   bias=mods[:, sh, 0:1], scale=gain[:, n, 0, k:k + 1]).then_inc(hf_ready, 1)
                    act.activation(h_f[k % 2][:, NS:T], x_n[k % 2][:, NS:T], ACT.Identity,
                                   bias=mods[:, sh, 1:2], scale=gain[:, n, 1, k:k + 1]).then_inc(hf_ready, 1)
                    act.wait_ge(hf_ready, 2 * (KD * n + k + 1))
                    act.activation(h_hi[:, k, :], h_f[k % 2][:, :], ACT.Copy).then_inc(hh_ready, 1)

            def ada_rows(b):
                act.wait_ge(ada_mm, 4 * b + 4)
                act.activation(a_row[0:2, :], misc[0:2, :], ACT.Copy).then_inc(ada_row, 1)

            act.wait_ge(vecs_ready, 2)
            act.activation(cond[:, :, 0], vecs[:, C_S:C_S + KD], ACT.Silu)
            act.activation(cond[:, :, 1], vecs[:, C_P:C_P + KD], ACT.Silu).then_inc(cond_ready, 1)
            for k in range(KD):
                act.wait_ge(x_tr, k + 1)
                act.activation(x[:, k, 0:NS], acc[k % 2][:, 0, :], ACT.Copy).then_inc(x_ready, 1)
                act.activation(x[:, k, NS:T], acc[k % 2][:, 1, 0:NP], ACT.Copy).then_inc(x_ready, 1)
                squares(0, k, lambda: act.wait_ge(x_ready, 2 * k + 2))
            split_hi(0, 0)
            act.wait_ge(gla_in_sem, 16 * 6)
            act.activation(g1_hi[:, :, :], g1_raw[:, :, :], ACT.Copy).then_inc(g1h, 1)
            act.wait_ge(ada_mm, 16)
            act.activation(a_first_row[0:2, 0:1024].rearrange("p (b n) -> p b n", b=2), work2[0:2, :, :], ACT.Copy)\
                .then_inc(ada_row, 2)
            norm_inv_sqrt(0, 0)
            modulate(0)
            act.wait_ge(zero_set, 2)
            act.wait_ge(g1_mm, 1)
            act.activation(z1[0:2 * RANK, :].rearrange("p (s n) -> p s n", s=2), acc[1][0:2 * RANK, :, 0:HALF],
                           ACT.Copy).then_inc(z1_ready, 1)

            def gate_logs(h, d, name):
                i = 2 * h + d
                act.wait_ge(work_mm, step(h, name) + 1)
                if not (isinstance(h, int) and h == 0):
                    act.wait_ge(work_mm, step(h - 1, ("Tf", "Tb")[d]) + 1)
                act.activation(za[d][:, :].rearrange("p (s n) -> p s n", s=2), work2[:, :, 0:HALF], ACT.Identity,
                               bias=vecs[:, bias_col(h, d)]).then_inc(work_free, 1)
                act.wait_ge(work_free, step(h, name) + 1)
                act.activation(zb[d][:, :], za[d][:, :], ACT.Abs).then_inc(z_step, 1)
                act.wait_ge(z_step, 3 * i + 1)
                act.activation(zb[d][:, :], zb[d][:, :], ACT.Exp, scale=-1.0).then_inc(z_step, 1)
                act.wait_ge(z_step, 3 * i + 2)
                act.activation(zb[d][:, :], zb[d][:, :], ACT.Ln, bias=1.0).then_inc(z_step, 1)

            def bias_col(h, d):
                return slice(B_G + 4 * d + h, B_G + 4 * d + h + 1)

            def decays(h, d):
                i = 2 * h + d
                act.wait_ge(scanned, i + 1)
                act.activation(za[d][:, :], zb[d][:, :], ACT.Exp, scale=1.0 / TAU).then_inc(e_ready, 1)
                act.activation(zb[d][:, :], zb[d][:, :], ACT.Exp, scale=-1.0 / TAU).then_inc(e_ready, 1)

            def read_acc(pair, slot, dst, func, src=None):
                src = acc[slot] if src is None else src
                act.wait_ge(unit_mm, unit(pair, slot) + 1)
                return act.activation(dst.rearrange("p (s n) -> p s n", s=2), src[:, :, 0:HALF], func)\
                    .then_inc(acc_free[slot], 1)

            def k_end_read(h, d, name):
                act.wait_ge(work_mm, step(h, name) + 1)
                if isinstance(h, int) and h == 0 and d == 0:
                    act.wait_ge(zero_set, 3)
                for cc in range(2):
                    rows = slice(cc * CH, (cc + 1) * CH)
                    op = act.activation(k_end[rows, :, cc, :], work_t[rows, :].rearrange("p (t n) -> p t n", t=NT),
                                        ACT.Copy)
                op.then_inc(work_free, 1)

            def o_squares(h, part):
                act.wait_ge(work_free, step(h, "Oa" if part == 0 else "Ob") + 1)
                for t in (range(4) if part == 0 else (4,)):
                    if NT * (h - 1) + t:
                        act.wait_ge(o_sq, NT * (h - 1) + t)
                    act.activation(sq_dump[:, :], o_tok[:, t, :], ACT.Square, accum_out=small[:, t:t + 1])\
                        .then_inc(o_sq, 1)

            def o_rstd(h):
                act.wait_ge(on_step, 4 * (h - 1) + 1)
                act.activation(small[:, 16:16 + NT], small[:, 8:8 + NT], ACT.Ln).then_inc(on_act, 1)
                act.wait_ge(on_act, 2 * (h - 1) + 1)
                act.activation(small[:, 16:16 + NT], small[:, 16:16 + NT], ACT.Exp, scale=-0.5).then_inc(on_act, 1)

            def gla_head(h):
                first = isinstance(h, int) and h == 0
                p = 3 * h
                split_hi(p, 1)
                gate_logs(h, 0, "Zf")
                if not first:
                    o_squares(h, 0)
                split_hi(p + 1, 0)
                if not first:
                    act.wait_ge(qd_ready, 2 * h)
                    act.wait_ge(kd_ready, 2 * h)
                read_acc(p, 0, q_t[:, :], ACT.Copy)
                if not first:
                    o_squares(h, 1)
                    o_rstd(h)
                blocks = ada_blocks_of(h)
                ada_rows(blocks[0])
                gate_logs(h, 1, "Zb")
                split_hi(p + 1, 1)
                read_acc(p, 1, k_t[:, :], ACT.Copy)
                decays(h, 0)
                split_hi(p + 2, 0)
                if not first:
                    act.wait_ge(work_mm, step(h - 1, "VT1") + 1)
                read_acc(p + 1, 0, v_t[:, :], ACT.Copy)
                decays(h, 1)
                split_hi(p + 2, 1)
                act.wait_ge(work_mm, step(h, "VT0") + 1)
                read_acc(p + 1, 1, v_t[:, :], ACT.Copy)
                k_end_read(h, 0, "Tf")
                split_hi(p + 3, 0)
                for b in blocks[1:]:
                    ada_rows(b)
                if not first:
                    act.wait_ge(work_free, step(h, "OT1") + 1)
                read_acc(p + 2, 0, r_s[:, 0, :], ACT.Silu)
                read_acc(p + 2, 1, r_s[:, 1, :], ACT.Silu)
                k_end_read(h, 1, "Tb")

            for h in range(GH):
                gla_head(h)
            ada_rows(ADA_TAIL)
            o_squares(GH, 0)
            o_squares(GH, 1)
            o_rstd(GH)
            ada_rows(ADA_TAIL + 1)

            def split_o(l, last_unit, tile_ready):
                act.wait_ge(unit_mm, last_unit)
                for k in range(KD):
                    tile_ready(k)
                    act.activation(h_hi[:, k, :], o_buf[:, k, :], ACT.Copy).then_inc(oh_ready, 1)

            split_o(0, unit(GLA_OUT, 0), lambda k: act.wait_ge(work_free, step(GH, "OT1") + 1))

            def projection(first, n, after):
                def one(i, last):
                    split_hi(first + i, 1)
                    if last:
                        after()
                    else:
                        split_hi(first + i + 1, 0)
                for i in range(KD // 2):
                    one(i, i == KD // 2 - 1)
                    for s in range(2):
                        k = 2 * i + s
                        squares(n, k, lambda: act.wait_ge(acc_free[s], first + i + 1))
                split_hi(first + KD // 2, 1)

            def ffn(layer, n, last_split, beside=None):
                for half in range(2):
                    first = FFN[layer] + half * FHALF
                    done = HT * (2 * layer + half)

                    def up(i, last, split_1=True):
                        if split_1:
                            split_hi(first + i, 1)
                        split_hi(first + i + 1, 0, HT if last else KD)
                        act.wait_ge(unit_mm, unit(first + i, 0) + 1)
                        act.wait_ge(acc_free[1], first + i)
                        act.activation(silu_g[:, :].rearrange("p (s n) -> p s n", s=2), acc[0][:, :, 0:HALF],
                                       ACT.Silu).then_inc(acc_free[0], 1)
                        act.wait_ge(acc_free[1], first + i + 1)
                        act.activation(hid_hi[:, bass.ds(i, 1), :].rearrange("p a n -> p (a n)"), hid_f[:, :],
                                       ACT.Copy).then_inc(hidh_ready, 1)
                    if half == 0:
                        if beside:
                            ada_rows(beside)
                        up(0, False, False)
                        with act.Fori(1, HT - 1) as i:
                            up(i, False)
                    else:
                        with act.Fori(0, HT - 1) as i:
                            up(i, False)
                    up(HT - 1, True)

                    def down(i, last):
                        split_hi(first + HT + i, 1, HT)
                        if last:
                            if half == 0:
                                split_hi(first + HT + i + 1, 0)
                            else:
                                last_split()
                        else:
                            split_hi(first + HT + i + 1, 0, HT)
                    for i in range(KD // 2):
                        down(i, i == KD // 2 - 1)
                        if half == 1:
                            for s in range(2):
                                k = 2 * i + s
                                squares(n + 1, k, lambda: act.wait_ge(acc_free[s], first + HT + i + 1))
                if layer == 0:
                    split_hi(DIF_IN, 1)

            ada_rows(ADA_TAIL + 2)
            projection(GLA_OUT, 1, lambda: split_hi(FFN[0], 0))
            norm_inv_sqrt(1, 1)
            ada_rows(ADA_NORM1)
            modulate(1)
            ffn(0, 1, lambda: split_hi(DIF_IN, 0), ADA_NORM1 + 1)
            norm_inv_sqrt(2, 2)
            ada_rows(ADA_NORM2)
            modulate(2)

            act.wait_ge(lam_step, 3)
            act.activation(small[:, 34:36], small[:, 32:34], ACT.Exp).then_inc(lam_step, 1)

            def done(g, name):
                act.wait_ge(buf_mm[buf_of(name)], count_of(g, name) + 1)
                return bufs[buf_of(name)]

            def operands(g):
                act.wait_ge(past_in, 32 * (g.n + 1))
                act.activation(vv_hi[:, 0:2, :], v_past[:, :, :], ACT.Copy).then_inc(past_hi, 1)
                act.wait_ge(rope_step, 6 * g.n + 3)
                if g.first:
                    act.wait_ge(q_zero, 4)
                for m in range(2):
                    rows = slice(m * DH, (m + 1) * DH)
                    act.activation(q_hi[rows, m, :], q_f[rows, :], ACT.Copy).then_inc(qs_hi, 1)
                act.wait_ge(rope_step, 6 * g.n + 6)
                act.activation(kk_hi[:, PAST:], k_f[:, :], ACT.Copy).then_inc(ks_hi, 1)
                if not g.first:
                    inv_sqrt(3 + g.n - 1, o_var[:, :], o_inv[:, :])
                out = done(g, "AD")
                if not g.first:
                    act.wait_ge(buf_mm[buf_of("AT")], count_of(g.before(), "AT") + 1)
                act.activation(a_row[0:2, :], out[0:2, 0:512], ACT.Copy).then_inc(buf_free[buf_of("AD")], 1)
                out = done(g, "VT")
                act.activation(vv_hi[:, 2:, :].rearrange("p t n -> p (t n)"), out[:, 0:T], ACT.Copy).then_inc(vt_hi, 1)
                out = done(g, "KC")
                act.activation(kk_hi[:, 0:PAST], out[:, 0:PAST], ACT.Copy).then_inc(kc_hi, 1)

            def exps(g, q, m):
                i = 2 * (NT * g.n + q) + m
                act.wait_ge(nm_ready, i + 1)
                if m == 1 and not (g.first and q < 2):
                    act.wait_ge(w_ready, NT * g.n + q - 1)
                name = f"S{q}{m}" if q < 4 else "SP"
                n = SK if q < 4 else P
                src = bufs[buf_of(name)][:, 0:n] if q < 4 else bufs[buf_of(name)][:, m * P:(m + 1) * P]
                op = act.activation((w_map, p1)[m][q % 2][:, 0:n], src, ACT.Exp, bias=stat[:, q, 2 + m:3 + m], scale=DH ** -0.5,
                                    accum_out=stat[:, q, 4 + m:5 + m])
                if q < 4 or m:
                    op.then_inc(buf_free[buf_of(name)], 1)

            def scaled(g, q):
                n = SK if q < 4 else P
                act.wait_ge(rc_step, 2 * (NT * g.n + q) + 1)
                act.activation(w_map[q % 2][:, 0:n], w_map[q % 2][:, 0:n], ACT.Copy, scale=stat[:, q, 6:7]).then_inc(t_ready, 1)

            def turned(g, q):
                out = done(g, f"T{q}" if q < 4 else "TP")
                if q < 4:
                    dst = wt_hi[q // 2][:, :, (q % 2) * P:(q % 2 + 1) * P]
                    src = out[:, 0:SK].rearrange("p (t n) -> p t n", n=P)
                else:
                    dst, src = wtp_hi[:, :], out[:, 0:P]
                act.activation(dst, src, ACT.Copy).then_inc(wt_up, 1)

            def o_read(g, pp):
                out = done(g, f"O{pp}")
                if not g.first and pp == 0:
                    act.wait_ge(ob_ready, g.n)
                op = act.activation(o_f[:, 2 * pp * P:2 * (pp + 1) * P], out[:, 0:2 * P], ACT.Copy)
                if pp:
                    op = act.activation(o_f[:, NS:T], out[:, 512:512 + P], ACT.Copy)
                op.then_inc(buf_free[buf_of(f"O{pp}")], 1)

            def unit_read(h, j):
                if not h.first:
                    if j == 0:
                        act.wait_ge(qs_lo, 2 * h.n)
                    elif j == 1:
                        act.wait_ge(ks_lo, h.n)
                        act.wait_ge(buf_mm[buf_of("KT")], count_of(h.before(), "KT") + 1)
                    else:
                        act.wait_ge(buf_mm[buf_of("VT")], count_of(h.before(), "VT") + 1)
                read_acc(*h.unit(j), (q_f, k_f, v_f)[j][:, :], ACT.Copy, acc[1 if h.first and j == 1 else 0])

            def next_split(h, j):
                split_hi(*h.unit(j + 1))

            def head(h):
                g = h.before() if h else LAST_HEAD
                unit_read(g, 2)
                if h:
                    next_split(h, 0)
                operands(g)
                if h:
                    unit_read(h, 0)
                    next_split(h, 1)
                exps(g, 0, 0)
                exps(g, 0, 1)
                exps(g, 1, 0)
                scaled(g, 0)
                exps(g, 1, 1)
                scaled(g, 1)
                turned(g, 0)
                exps(g, 2, 0)
                exps(g, 2, 1)
                if h:
                    unit_read(h, 1)
                scaled(g, 2)
                turned(g, 1)
                if h:
                    next_split(h, 2)
                exps(g, 3, 0)
                exps(g, 3, 1)
                o_read(g, 0)
                scaled(g, 3)
                turned(g, 2)
                exps(g, 4, 0)
                exps(g, 4, 1)
                turned(g, 3)
                scaled(g, 4)
                turned(g, 4)
                o_read(g, 1)
                act.wait_ge(buf_free[buf_of("O1")], count_of(g, "O1") + 1)
                act.activation(o_sqr[:, :], o_f[:, :], ACT.Square).then_inc(os_ready, 1)

            unit_read(Head(0, 0), 0)
            next_split(Head(0, 0), 1)
            unit_read(Head(0, 0), 1)
            next_split(Head(0, 0), 2)
            head(Head(0, 1))
            with act.Fori(1, AH // 2) as i:
                for odd in range(2):
                    head(Head(i, odd))
            head(None)
            act.wait_ge(buf_free[buf_of("SS")], count_of(LAST_HEAD, "SS") + 1)
            inv_sqrt(3 + AH - 1, o_var[:, :], o_inv[:, :])

            split_o(1, unit(DIF_OUT, 0), lambda k: act.wait_ge(ob_ready, k + 1))
            projection(DIF_OUT, 3, lambda: split_hi(FFN[1], 0))
            norm_inv_sqrt(3 + AH, 3)
            modulate(3)
            ffn(1, 3, lambda: None)
            norm_inv_sqrt(4 + AH, 4)
            for k in range(KD):
                act.wait_ge(y_mm, k + 1)
                act.activation(y_tok[:, 0:NS // P, k * P:(k + 1) * P],
                               acc[k % 2][:, 0, :].rearrange("p (t n) -> p t n", n=P), ACT.Copy).then_inc(y_copied, 1)
                act.activation(y_tok[:, NS // P, k * P:(k + 1) * P], acc[k % 2][:, 1, 0:P], ACT.Copy)\
                    .then_inc(y_copied, 1)

        @block.vector
        def _(dve):
            def split_lo(pair, slot, kt=KD):
                dve.wait_ge(hi_ready, unit(pair, slot) + 1)
                dve.tensor_tensor(w_lo[slot][:, 0:kt * P], w_raw[slot][:, 0:kt * P],
                                  w_hi[slot][:, 0:kt * P].bitcast(F32), ALU.subtract).then_inc(lo_ready, 1)

            def add_squares(n, k):
                if k in (0, KD - 1):
                    return
                dve.wait_ge(sq_ready, KD * n + k + 1)
                if not (n == 0 and k == 1):
                    dve.wait_ge(sq_added, (KD - 2) * n + k - 1)
                dve.tensor_tensor(sq_acc[:, :], sq_acc[:, :], sq[k % 2][:, :], ALU.add).then_inc(sq_added, 1)

            def variance(n, v, sums=work2):
                dve.wait_ge(ss_mm, n + 1)
                dve.tensor_scalar(v.rearrange("p (s n) -> p s n", s=2), sums[:, :, 0:HALF], 1.0 / D, EPS,
                                  ALU.mult, ALU.add).then_inc(var_ready, 1)

            def newton_step(m, v, y, t):
                dve.wait_ge(y0_ready, m + 1)
                dve.scalar_tensor_tensor(out=t, in0=y, scalar=-0.5, in1=y, op0=ALU.mult, op1=ALU.mult)\
                    .then_inc(newton, 1)
                dve.wait_ge(newton, 3 * m + 1)
                dve.tensor_tensor(t, t, v, ALU.mult).then_inc(newton, 1)
                dve.wait_ge(newton, 3 * m + 2)
                dve.scalar_tensor_tensor(out=y, in0=t, scalar=1.5, in1=y, op0=ALU.add, op1=ALU.mult)\
                    .then_inc(newton, 1)

            def mods_ready(blocks):
                if blocks <= ADA_DIF:
                    dve.wait_ge(ada_mod, blocks)
                else:
                    g = blocks - 1 - ADA_DIF
                    dve.wait_ge(buf_free[buf_of("AT")], count_of(Head(g // 2, g % 2), "AT") + 1)

            def gains(n):
                l, part = n // 2, n % 2
                sc = l * 48 + (3 * part + 1) * 8
                g0 = (G_MIX, G_FFN)[part] + l * KD
                mods_ready(AB * l + (4, 10)[part])
                for v in range(2):
                    dve.scalar_tensor_tensor(out=gain[:, n, v, :], in0=mods[:, sc:sc + KD, v], scalar=1.0,
                                             in1=vecs[:, g0:g0 + KD], op0=ALU.add, op1=ALU.mult)\
                        .then_inc(gain_ready, 1)

            def modulate(n, m):
                for k in range(KD + 1):
                    if k < KD:
                        dve.wait_ge(newton, 3 * m + 3)
                        if k >= 2:
                            dve.wait_ge(hf_ready, 2 * (KD * n + k - 1))
                        dve.tensor_tensor(x_n[k % 2][:, :], x[:, k, :], rstd[:, :], ALU.mult).then_inc(xn_ready, 1)
                    if k >= 1:
                        dve.wait_ge(hh_ready, KD * n + k)
                        dve.tensor_tensor(h_lo[:, k - 1, :], h_f[(k - 1) % 2][:, :], h_hi[:, k - 1, :].bitcast(F32),
                                          ALU.subtract).then_inc(h_ready, 1)

            def ada_mods(b):
                dve.wait_ge(ada_t, b + 1)
                dst = mods[:, 4 * b:4 * b + 4, :] if isinstance(b, int) else mods[:, bass.ds(4 * b, 4), :]
                bias = mod_bias[:, 4 * b:4 * b + 4] if isinstance(b, int) else mod_bias[:, bass.ds(4 * b, 4)]
                dve.tensor_tensor(dst, misc[:, 0:8].rearrange("p (j v) -> p j v", v=2),
                                  bias.unsqueeze(2).to_broadcast([P, 4, 2]), ALU.add).then_inc(ada_mod, 1)

            dve.memset(ones[:, :], 1.0).then_inc(ones_set, 1)
            dve.wait_ge(rows_t, 2)
            dve.tensor_copy(mod_bias[:, :], misc[:, 0:96]).then_inc(vecs_ready, 1)
            dve.tensor_copy(vecs[:, :], misc[:, 128:128 + 67]).then_inc(vecs_ready, 1)
            for k in range(1, KD):
                add_squares(0, k)
            split_lo(0, 0)
            dve.wait_ge(g1h, 1)
            dve.tensor_tensor(g1_lo[:, :, :], g1_raw[:, :, :], g1_hi[:, :, :].bitcast(F32), ALU.subtract)\
                .then_inc(g1l, 1)
            dve.wait_ge(ada_mm, 16)
            dve.tensor_copy(a_first_row[0:2, 1024:2048].rearrange("p (b n) -> p b n", b=2), side[0:2, :, :])\
                .then_inc(ada_row, 2)
            variance(0, var[:, :], acc[0])
            newton_step(0, var[:, :], rstd[:, :], sq[0][:, :])
            dve.wait_ge(ada_t, 4)
            dve.tensor_tensor(mods[:, 0:16, :], acc[1][:, 0, 0:32].rearrange("p (j v) -> p j v", v=2),
                              mod_bias[:, 0:16].unsqueeze(2).to_broadcast([P, 16, 2]), ALU.add).then_inc(ada_mod, 4)
            gains(0)
            modulate(0, 0)

            def log_decay(h, d):
                i = 2 * h + d
                dve.wait_ge(z_step, 3 * i + 3)
                dve.scalar_tensor_tensor(out=za[d][:, :], in0=za[d][:, :], scalar=0.0, in1=zb[d][:, :],
                                         op0=ALU.min, op1=ALU.subtract).then_inc(log_a, 1)
                dve.wait_ge(log_a, i + 1)
                src, dst = (za[d][:, :], zb[d][:, :]) if d == 0 else (za[d][:, ::-1], zb[d][:, ::-1])
                dve.tensor_tensor_scan(dst, chunk_mask[:, :], src, 0.0, ALU.mult, ALU.add).then_inc(scanned, 1)

            def decayed(h, d):
                i = 2 * h + d
                dve.wait_ge(e_ready, 2 * i + 2)
                dve.wait_ge(acc_free[0], 3 * h + 1)
                dve.wait_ge(acc_free[1], 3 * h + 1)
                if not (isinstance(h, int) and h == 0):
                    dve.wait_ge(work_mm, step(h, "Ob") + 1)
                dve.scalar_tensor_tensor(out=q_d[d][:, :], in0=q_t[:, :], scalar=DK ** -0.5, in1=za[d][:, :],
                                         op0=ALU.mult, op1=ALU.mult).then_inc(qd_ready, 1)
                dve.tensor_tensor(k_d[d][:, :], k_t[:, :], zb[d][:, :], ALU.mult).then_inc(kd_ready, 1)
                last = za[d][:, :].rearrange("p (n c) -> p n c", c=CH)[:, :, CH - 1 if d == 0 else 0]
                dve.tensor_copy(decay[:, d, :], last).then_inc(dec_ready, 1)
                dve.wait_ge(dec_ready, i + 1)
                dve.wait_ge(kd_ready, i + 1)
                dve.tensor_tensor(za[d][:, :].rearrange("p (n c) -> p n c", c=CH),
                                  k_d[d][:, :].rearrange("p (n c) -> p n c", c=CH),
                                  decay[:, d, :].unsqueeze(2).to_broadcast([P, NCH, CH]), ALU.mult)\
                    .then_inc(ke_ready, 1)

            def masked(h, d, name):
                dve.wait_ge(work_mm, step(h, name) + 1)
                if h == 0 and d == 0:
                    dve.wait_ge(gla_in_sem, 16 * 6)
                dst = attn if d == 0 else zb[1]
                dve.tensor_tensor(dst[:, :].rearrange("p (t n) -> p t n", t=NT),
                                  work_t.rearrange("p (t n) -> p t n", t=NT),
                                  mask[:, d, :].unsqueeze(1).to_broadcast([P, NT, P]), ALU.mult)\
                    .then_inc(work_free, 1)
                if d == 0:
                    return
                dve.wait_ge(work_free, step(h, name) + 1)
                dve.tensor_tensor(attn[:, :], attn[:, :], zb[1][:, :], ALU.add).then_inc(attn_ready, 1)

            def v_read(h, j, name):
                dve.wait_ge(work_mm, step(h, name) + 1)
                dve.tensor_copy(v_tok[:, :, j * P:(j + 1) * P], work_t.rearrange("p (t n) -> p t n", t=NT))\
                    .then_inc(work_free, 1)

            def states(h, d):
                if h >= 1:
                    dve.wait_ge(st_out[d], 16 * h)
                dve.wait_ge(st_in, 32 * (h + 1))
                for i, n in enumerate((DS_F, DS_B)[d]):
                    number = 2 * NDS * h + NDS * d + i
                    dve.wait_ge(ds_mm, (NDS + 1) * h + (NDS + 1) // 2 * d + i // 2 + 1)
                    before = state_in(d, n)
                    if before is None:
                        dve.tensor_copy(state_out(d, n), spare[:, i % 2, :]).then_inc(st_upd, 1)
                    else:
                        if number:
                            dve.wait_ge(st_upd, number)
                        dve.scalar_tensor_tensor(out=state_out(d, n), in0=before, scalar=decay[:, d, n:n + 1],
                                                 in1=spare[:, i % 2, :], op0=ALU.mult, op1=ALU.add)\
                            .then_inc(st_upd, 1)

            def o_copy(h, part):
                dve.wait_ge(work_mm, step(h, "Oa" if part == 0 else "Ob") + 1)
                for t in (range(4) if part == 0 else (4,)):
                    op = dve.tensor_copy(o_tok[:, t, :], work[:, t % 4, :])
                op.then_inc(work_free, 1)

            def o_norm(h):
                g = h - 1
                v, y, t = small[:, 8:8 + NT], small[:, 16:16 + NT], small[:, 24:24 + NT]
                dve.wait_ge(o_sq, NT * h)
                dve.tensor_scalar(v, small[:, 0:NT], 1.0 / DV, EPS, ALU.mult, ALU.add).then_inc(on_step, 1)
                dve.wait_ge(on_act, 2 * g + 2)
                dve.scalar_tensor_tensor(out=t, in0=y, scalar=-0.5, in1=y, op0=ALU.mult, op1=ALU.mult)\
                    .then_inc(on_step, 1)
                dve.wait_ge(on_step, 4 * g + 2)
                dve.tensor_tensor(t, t, v, ALU.mult).then_inc(on_step, 1)
                dve.wait_ge(on_step, 4 * g + 3)
                dve.scalar_tensor_tensor(out=y, in0=t, scalar=1.5, in1=y, op0=ALU.add, op1=ALU.mult)\
                    .then_inc(on_step, 1)
                dve.wait_ge(on_step, 4 * g + 4)
                for tt in range(NT):
                    op = dve.tensor_scalar(o_tok[:, tt, :], o_tok[:, tt, :], small[:, 16 + tt:17 + tt], None, ALU.mult)
                op.then_inc(o_scaled, 1)

            def o_gate(h, j, name):
                g = h - 1
                dve.wait_ge(work_mm, step(h, name) + 1)
                dve.wait_ge(acc_free[0], 3 * h)
                dve.wait_ge(acc_free[1], 3 * h)
                dve.scalar_tensor_tensor(out=o_buf[:, 2 * g + j, :], in0=work_t, scalar=vecs[:, G_GH + j:G_GH + j + 1],
                                         in1=r_s[:, j, :], op0=ALU.mult, op1=ALU.mult).then_inc(work_free, 1)

            def gla_head(h):
                p = 3 * h
                first = h == 0
                split_lo(p, 1)
                if not first:
                    states(h - 1, 1)
                log_decay(h, 0)
                if not first:
                    o_copy(h, 0)
                split_lo(p + 1, 0)
                if not first:
                    o_copy(h, 1)
                    o_norm(h)
                split_lo(p + 1, 1)
                decayed(h, 0)
                blocks = ada_blocks_of(h)
                ada_mods(blocks[0])
                log_decay(h, 1)
                if not first:
                    o_gate(h, 0, "OT0")
                split_lo(p + 2, 0)
                masked(h, 0, "Af")
                if not first:
                    o_gate(h, 1, "OT1")
                decayed(h, 1)
                split_lo(p + 2, 1)
                v_read(h, 0, "VT0")
                split_lo(p + 3, 0)
                v_read(h, 1, "VT1")
                states(h, 0)
                masked(h, 1, "Ab")
                for b in blocks[1:]:
                    ada_mods(b)

            for h in range(GH):
                gla_head(h)
            states(GH - 1, 1)
            o_copy(GH, 0)
            ada_mods(ADA_TAIL)
            o_copy(GH, 1)
            o_norm(GH)
            o_gate(GH, 0, "OT0")
            o_gate(GH, 1, "OT1")
            ada_mods(ADA_TAIL + 1)

            def split_o(l):
                for k in range(KD):
                    dve.wait_ge(oh_ready, KD * l + k + 1)
                    dve.tensor_tensor(h_lo[:, k, :], o_buf[:, k, :], h_hi[:, k, :].bitcast(F32), ALU.subtract)\
                        .then_inc(ol_ready, 1)
            split_o(0)

            def add_to_x(pair, slot, k, part):
                dve.wait_ge(unit_mm, unit(pair, slot) + 1)
                g = part * 8 + k
                one = bass.ds(g, 1) if not isinstance(g, int) else slice(g, g + 1)
                xk = x[:, k, :] if isinstance(k, int) else x[:, bass.ds(k, 1), :].rearrange("p a n -> p (a n)")
                for half, lo, hi, v in ((0, 0, HALF, 0), (1, HALF, NS, 0), (1, NS, T, 1)):
                    op = dve.scalar_tensor_tensor(out=xk[:, lo:hi],
                                                  in0=acc[slot][:, half, lo - half * HALF:hi - half * HALF],
                                                  scalar=mods[:, one, v], in1=xk[:, lo:hi],
                                                  op0=ALU.mult, op1=ALU.add)
                op.then_inc(acc_free[slot], 1)

            def projection(first, l, n, after, beside=None):
                mods_ready(AB * l + 6)
                for i in range(KD // 2):
                    split_lo(first + i, 1)
                    if i < KD // 2 - 1:
                        split_lo(first + i + 1, 0)
                    else:
                        after()
                    for s in range(2):
                        add_to_x(first + i, s, 2 * i + s, l * 6 + 2)
                        add_squares(n, 2 * i + s)
                    if beside and i == 0:
                        ada_mods(beside)
                split_lo(first + KD // 2, 1)

            def ffn(layer, n, last_split, beside=None):
                for half in range(2):
                    first = FFN[layer] + half * FHALF
                    done = HT * (2 * layer + half)

                    def up(i, last, split_1=True):
                        if split_1:
                            split_lo(first + i, 1)
                        split_lo(first + i + 1, 0, HT if last else KD)
                        dve.wait_ge(acc_free[0], first + i + 1)
                        dve.wait_ge(unit_mm, unit(first + i, 1) + 1)
                        dve.tensor_tensor(hid_f[:, :].rearrange("p (s n) -> p s n", s=2),
                                          silu_g[:, :].rearrange("p (s n) -> p s n", s=2), acc[1][:, :, 0:HALF],
                                          ALU.mult).then_inc(acc_free[1], 1)
                        dve.wait_ge(acc_free[1], first + i + 1)
                        dve.wait_ge(hidh_ready, done + i + 1)
                        dst = hid_lo[:, bass.ds(i, 1), :].rearrange("p a n -> p (a n)")
                        up_part = hid_hi[:, bass.ds(i, 1), :].rearrange("p a n -> p (a n)").bitcast(F32)
                        dve.tensor_tensor(dst, hid_f[:, :], up_part, ALU.subtract).then_inc(hidl_ready, 1)
                    if half == 0:
                        up(0, False, False)
                        if beside:
                            ada_mods(beside)
                    with dve.Fori(1 - half, HT - 1) as i:
                        up(i, False)
                    up(HT - 1, True)
                    if half == 0:
                        mods_ready(AB * layer + 12)
                    for i in range(KD // 2):
                        split_lo(first + HT + i, 1, HT)
                        if i < KD // 2 - 1:
                            split_lo(first + HT + i + 1, 0, HT)
                        elif half == 0:
                            split_lo(first + HT + i + 1, 0)
                        else:
                            last_split()
                        for s in range(2):
                            add_to_x(first + HT + i, s, 2 * i + s, layer * 6 + 5)
                            if half == 1:
                                add_squares(n + 1, 2 * i + s)
                if layer == 0:
                    split_lo(DIF_IN, 1)

            projection(GLA_OUT, 0, 1, lambda: split_lo(FFN[0], 0), ADA_TAIL + 2)
            variance(1, var[:, :])
            newton_step(1, var[:, :], rstd[:, :], sq[0][:, :])
            ada_mods(ADA_NORM1)
            gains(1)
            modulate(1, 1)
            ffn(0, 1, lambda: split_lo(DIF_IN, 0), ADA_NORM1 + 1)
            variance(2, var[:, :])
            newton_step(2, var[:, :], rstd[:, :], sq[0][:, :])
            ada_mods(ADA_NORM2)
            gains(2)
            modulate(2, 2)

            dve.wait_ge(dif_in, 16 * 5)
            dve.tensor_tensor(lam_in[:, 0, :], lam_in[:, 0, :], lam_in[:, 1, :], ALU.mult).then_inc(lam_step, 1)
            dve.wait_ge(lam_step, 1)
            dve.tensor_reduce(small[:, 32:34], lam_in[:, 0, :].rearrange("p (m d) -> p m d", m=2), AX_X, ALU.add)\
                .then_inc(lam_step, 1)
            dve.tensor_scalar(small[:, 36:37], vecs[:, G_DH:G_DH + 1], 1.0 - LAM_INIT, None, ALU.mult)\
                .then_inc(lam_step, 1)
            dve.wait_ge(lam_step, 4)
            dve.scalar_tensor_tensor(out=lam_neg[:, :], in0=small[:, 35:36], scalar=LAM_INIT, in1=small[:, 34:35],
                                     op0=ALU.subtract, op1=ALU.subtract).then_inc(lam_ready, 1)
            dve.wait_ge(lam_ready, 1)
            g_dif = small[:, 36:37]

            def done(g, name):
                dve.wait_ge(buf_mm[buf_of(name)], count_of(g, name) + 1)
                return bufs[buf_of(name)]

            def rope(g, j, name, src):
                i = 6 * g.n + 3 * j
                pair, slot = g.unit(j)
                dve.wait_ge(acc_free[slot], pair + 1)
                dve.tensor_tensor(roped[:, :], src[:, 0:NS], cos_t[:, :], ALU.mult).then_inc(rope_step, 1)
                out = done(g, name)
                dve.wait_ge(rope_step, i + 1)
                dve.tensor_tensor(src[:, 0:NS], out[:, 0:NS], sin_t[:, :], ALU.mult).then_inc(buf_free[buf_of(name)], 1)
                dve.wait_ge(buf_free[buf_of(name)], count_of(g, name) + 1)
                dve.tensor_tensor(src[:, 0:NS], src[:, 0:NS], roped[:, :], ALU.add).then_inc(rope_step, 2)
                dve.wait_ge(rope_step, i + 3)

            def finish(g):
                m = 3 + g.n
                newton_step(m, o_var[:, :], o_inv[:, :], o_sqr[:, :])
                dve.wait_ge(newton, 3 * m + 3)
                dve.scalar_tensor_tensor(out=o_buf[:, bass.ds(g.n, 1), :].rearrange("p a n -> p (a n)"), in0=o_f[:, :],
                                         scalar=g_dif, in1=o_inv[:, :],
                                         op0=ALU.mult, op1=ALU.mult).then_inc(ob_ready, 1)

            def operands(g):
                rope(g, 0, "Rq", q_f)
                for m in range(2):
                    rows = slice(m * DH, (m + 1) * DH)
                    dve.wait_ge(qs_hi, 2 * g.n + m + 1)
                    if g.first:
                        dve.wait_ge(q_zero, 4)
                    dve.tensor_tensor(q_lo[rows, m, :], q_f[rows, :], q_hi[rows, m, :].bitcast(F32), ALU.subtract)\
                        .then_inc(qs_lo, 1)
                rope(g, 1, "Rk", k_f)
                dve.wait_ge(ks_hi, g.n + 1)
                dve.tensor_tensor(kk_lo[:, PAST:], k_f[:, :], kk_hi[:, PAST:].bitcast(F32), ALU.subtract)\
                    .then_inc(ks_lo, 1)
                dve.wait_ge(past_hi, g.n + 1)
                dve.tensor_tensor(vv_lo[:, 0:2, :], v_past[:, :, :], vv_hi[:, 0:2, :].bitcast(F32), ALU.subtract)\
                    .then_inc(past_lo, 1)
                if not g.first:
                    finish(g.before())
                dve.wait_ge(vt_hi, g.n + 1)
                out = bufs[buf_of("VT")]
                if not g.first:
                    dve.wait_ge(kv_out, 16 * g.n)
                dve.tensor_copy(v_new[:, :], out[:, NS:T]).then_inc(v_out, 1)
                dve.tensor_tensor(vv_lo[:, 2:, :].rearrange("p t n -> p (t n)"), out[:, 0:T],
                                  vv_hi[:, 2:, :].rearrange("p t n -> p (t n)").bitcast(F32), ALU.subtract)\
                    .then_inc(buf_free[buf_of("VT")], 1)
                dve.wait_ge(kc_hi, g.n + 1)
                out = bufs[buf_of("KC")]
                dve.tensor_tensor(kk_lo[:, 0:PAST], out[:, 0:PAST], kk_hi[:, 0:PAST].bitcast(F32), ALU.subtract)\
                    .then_inc(buf_free[buf_of("KC")], 1)
                out = done(g, "KT")
                if not g.first:
                    dve.wait_ge(k_out, 16 * g.n)
                dve.tensor_copy(k_new[:, :], out[:, 0:P]).then_inc(buf_free[buf_of("KT")], 1)
                out = done(g, "AT")
                b = ADA_DIF + g.n
                dve.tensor_tensor(mods[:, bass.ds(b * 4, 4), :], out[:, 0:8].rearrange("p (j v) -> p j v", v=2),
                                  mod_bias[:, bass.ds(b * 4, 4)].unsqueeze(2).to_broadcast([P, 4, 2]), ALU.add)\
                    .then_inc(buf_free[buf_of("AT")], 1)

            def maxima(g, q, m):
                i = 2 * (NT * g.n + q) + m
                if q < 4:
                    out = done(g, f"S{q}{m}")
                    dve.tensor_reduce(stat[:, q, m:m + 1], out[:, 0:SK], AX_X, ALU.max).then_inc(mx_done, 1)
                    dve.wait_ge(mx_done, i + 1)
                    dve.tensor_scalar(stat[:, q, 2 + m:3 + m], stat[:, q, m:m + 1], -DH ** -0.5, None, ALU.mult)\
                        .then_inc(nm_ready, 1)
                else:
                    out = done(g, "SP")
                    dve.tensor_reduce(stat[:, q, 0:2], out[:, 0:2 * P].rearrange("p (m n) -> p m n", m=2), AX_X, ALU.max)\
                        .then_inc(mx_done, 2)
                    dve.wait_ge(mx_done, i + 2)
                    dve.tensor_scalar(stat[:, q, 2:4], stat[:, q, 0:2], -DH ** -0.5, None, ALU.mult)\
                        .then_inc(nm_ready, 2)

            def norms(g, q):
                i = NT * g.n + q
                name = f"S{q}1" if q < 4 else "SP"
                dve.wait_ge(buf_free[buf_of(name)], count_of(g, name) + 1)
                dve.reciprocal(stat[:, q, 6:8], stat[:, q, 4:6]).then_inc(rc_step, 1)
                dve.wait_ge(rc_step, 2 * i + 1)
                dve.tensor_tensor(stat[:, q, 8:9], stat[:, q, 7:8], lam_neg[:, :], ALU.mult).then_inc(rc_step, 1)

            def combine(g, q):
                n = SK if q < 4 else P
                i = NT * g.n + q
                dve.wait_ge(t_ready, i + 1)
                dve.wait_ge(rc_step, 2 * i + 2)
                dve.scalar_tensor_tensor(out=w_map[q % 2][:, 0:n], in0=p1[q % 2][:, 0:n], scalar=stat[:, q, 8:9],
                                         in1=w_map[q % 2][:, 0:n], op0=ALU.mult, op1=ALU.add).then_inc(w_ready, 1)

            def turned(g, q):
                name = f"T{q}" if q < 4 else "TP"
                out = bufs[buf_of(name)]
                dve.wait_ge(wt_up, NT * g.n + q + 1)
                if q < 4:
                    at = slice((q % 2) * P, (q % 2 + 1) * P)
                    dst, up = wt_lo[q // 2][:, :, at], wt_hi[q // 2][:, :, at].bitcast(F32)
                    src = out[:, 0:SK].rearrange("p (t n) -> p t n", n=P)
                else:
                    dst, up, src = wtp_lo[:, :], wtp_hi[:, :].bitcast(F32), out[:, 0:P]
                dve.tensor_tensor(dst, src, up, ALU.subtract).then_inc(buf_free[buf_of(name)], 1)

            def next_split(h, j):
                split_lo(*h.unit(j + 1))

            def head(h):
                g = h.before() if h else LAST_HEAD
                if h:
                    next_split(h, 0)
                operands(g)
                if h:
                    next_split(h, 1)
                maxima(g, 0, 0)
                maxima(g, 0, 1)
                maxima(g, 1, 0)
                norms(g, 0)
                combine(g, 0)
                maxima(g, 1, 1)
                norms(g, 1)
                maxima(g, 2, 0)
                combine(g, 1)
                turned(g, 0)
                maxima(g, 2, 1)
                maxima(g, 3, 0)
                norms(g, 2)
                turned(g, 1)
                if h:
                    next_split(h, 2)
                combine(g, 2)
                maxima(g, 3, 1)
                norms(g, 3)
                maxima(g, 4, 0)
                combine(g, 3)
                turned(g, 2)
                norms(g, 4)
                turned(g, 3)
                combine(g, 4)
                turned(g, 4)
                out = done(g, "SS")
                dve.tensor_scalar(o_var[:, :].rearrange("p (s n) -> p s n", s=2), buf2[buf_of("SS")][:, :, 0:HALF],
                                  1.0 / (2 * DH), EPS, ALU.mult, ALU.add).then_inc(buf_free[buf_of("SS")], 1)

            next_split(Head(0, 0), 1)
            next_split(Head(0, 0), 2)
            head(Head(0, 1))
            with dve.Fori(1, AH // 2) as i:
                for odd in range(2):
                    head(Head(i, odd))
            head(None)
            finish(LAST_HEAD)
            split_o(1)
            projection(DIF_OUT, 1, 3, lambda: split_lo(FFN[1], 0))
            variance(3, var[:, :])
            newton_step(3 + AH, var[:, :], rstd[:, :], sq[0][:, :])
            gains(3)
            modulate(3, 3 + AH)
            ffn(1, 3, lambda: None)
            variance(4, var[:, :])
            newton_step(4 + AH, var[:, :], rstd[:, :], sq[0][:, :])
            dve.wait_ge(newton, 3 * (4 + AH) + 3)
            for k in range(KD):
                if k >= 2:
                    dve.wait_ge(y_mm, k - 1)
                dve.scalar_tensor_tensor(out=y_t[k % 2][:, :], in0=x[:, k, :], scalar=vecs[:, G_FIN + k:G_FIN + k + 1],
                                         in1=rstd[:, :], op0=ALU.mult, op1=ALU.mult).then_inc(y_ready, 1)


_INS = ["x_prompt", "x_sample", "state_gla_fwd", "state_gla_bwd", "cache_diff_k", "cache_diff_v", "c", "c_ctx", "w_ada",
        "b_ada", "g_mix_norm", "g_ffn_norm", "w_gla_in", "w_gla_g1", "w_gla_g2", "b_gla_g", "g_gla_head", "w_gla_out",
        "w_diff_qkv", "lam_q", "lam_k", "g_diff_head", "w_diff_out", "w_ffn_gate", "w_ffn_up", "w_ffn_down", "g_final"]
_OUTS = [(1, NP, D), (1, NS, D), (1, 1, GH, DK, DV), (1, 1, GH, DK, DV), (1, 1, NP, AH, 2, DH), (1, 1, NP, AH, 2 * DH)]


def shape_constants():
    import numpy as np
    f32 = np.float32
    i, j = np.arange(P)[:, None], np.arange(P)[None, :]
    same = i // CH == j // CH
    parts = [(i == j), same & (i <= j), same & (i >= j)]
    scan = np.broadcast_to(np.arange(T) % CH != 0, (P, T))
    half = DH // 2
    rot = np.where(i == j + half, -1.0, 0.0) * (j % DH < half) + np.where(i == j - half, 1.0, 0.0) * (j % DH >= half)
    n_freq = DH // 4
    inv = (f32(10000.0) ** (-np.arange(n_freq, dtype=f32) / f32(n_freq))).astype(f32)
    tok = np.arange(NS)
    ang = np.concatenate([(tok // 64).astype(f32)[:, None] * inv, (tok % 64).astype(f32)[:, None] * inv], axis=-1)
    tab = ang.T[np.arange(P) % DH % half]
    return np.ascontiguousarray(np.concatenate([a.astype(f32) for a in parts + [scan, rot, np.cos(tab), np.sin(tab)]],
                                               axis=1))


def kernel(**inputs):
    import numpy as _np
    import concourse.bacc as _bacc
    from concourse.bass_utils import run_bass_kernel_spmd as _run

    nc = _bacc.Bacc("TRN2", target_bir_lowering=False, num_devices=1, dynamic_dma_scratch_size=4096)
    arrays, args = {}, []
    for name in _INS:
        a = _np.ascontiguousarray(inputs[name])
        arrays[f"in_{name}_dram"] = a
        args.append(nc.dram_tensor(f"in_{name}_dram", a.shape, mybir.dt.from_np(a.dtype), kind="ExternalInput").ap())
    arrays["consts_dram"] = shape_constants()
    args.append(nc.dram_tensor("consts_dram", arrays["consts_dram"].shape, F32, kind="ExternalInput").ap())
    for i, shape in enumerate(_OUTS):
        args.append(nc.dram_tensor(f"out_{i}_dram", shape, F32, kind="ExternalOutput").ap())
    program(nc, *args)
    r = _run(nc, [arrays], core_ids=[0])
    return tuple(r.results[0][f"out_{i}_dram"] for i in range(len(_OUTS)))
```
